# Optimizing a Trainium2 kernel written in Bass

```python
import jax, jax.numpy as jnp
from jax import lax
import numpy as np

D_MODEL = 1024
BATCH = 1
SEQ = 1024
DEPTH = 1
DEC_BATCH = 8
DEC_SEQ = 1
PAST_LEN = 2048
PAGE_SIZE = 128

N_HEADS = 16
HEAD_DIM = 64
N_KV_HEADS = 4
GROUP = N_HEADS // N_KV_HEADS
ATTN_WIDTH = N_HEADS * HEAD_DIM
KV_WIDTH = N_KV_HEADS * HEAD_DIM
WINDOW = 128
ATTN_BLOCK = WINDOW
ATTN_SCALE = HEAD_DIM ** -0.5
NEG_BIG = -1e30
SGU_CHUNK = 128
SGU_WIDTH = D_MODEL
SGU_GROUPS = 8
SGU_GROUP_DIM = SGU_WIDTH // SGU_GROUPS
D_FF = 4 * D_MODEL
EPS = 1e-6
IN_SIZES = (SGU_WIDTH, SGU_WIDTH, ATTN_WIDTH, KV_WIDTH, KV_WIDTH, D_MODEL, D_MODEL)
IN_WIDTH = sum(IN_SIZES)
IN_OFFSETS = tuple(int(o) for o in np.cumsum(IN_SIZES)[:-1])

kernel_name = "hybrid_gated_sgu_swa_decoder_step"

def rmsnorm(x, g):
    xf = x.astype(jnp.float32)
    y = xf * lax.rsqrt(jnp.mean(xf * xf, axis=-1, keepdims=True) + EPS)
    return (y * g.astype(jnp.float32)).astype(x.dtype)

def alibi_slopes():
    h = jnp.arange(1, N_HEADS + 1, dtype=jnp.float32)
    return jnp.exp2(-8.0 * h / N_HEADS)

def in_proj(x, ln1_g, w_in):
    xn = rmsnorm(x, ln1_g)
    h = xn @ w_in
    u, v, q, k, va, ga, gb = jnp.split(h, IN_OFFSETS, axis=-1)
    u = jax.nn.gelu(u)
    v = jax.nn.gelu(v)
    lead = x.shape[:-1]
    q = q.reshape(lead + (N_KV_HEADS, GROUP, HEAD_DIM))
    k = k.reshape(lead + (N_KV_HEADS, HEAD_DIM))
    va = va.reshape(lead + (N_KV_HEADS, HEAD_DIM))
    return u, v, q, k, va, ga, gb

def sink_attend(q, k, v, dist, valid, sinks, slopes):
    s = jnp.einsum('...qhgd,...shd->...hgqs', q, k).astype(jnp.float32) * ATTN_SCALE
    s = s - slopes.reshape(N_KV_HEADS, GROUP, 1, 1) * dist.astype(jnp.float32)
    s = jnp.where(valid, s, NEG_BIG)
    sink = jnp.broadcast_to(sinks.astype(jnp.float32).reshape(N_KV_HEADS, GROUP, 1, 1), s.shape[:-1] + (1,))
    p = jax.nn.softmax(jnp.concatenate([s, sink], axis=-1), axis=-1)[..., :-1]
    return jnp.einsum('...hgqs,...shd->...qhgd', p.astype(v.dtype), v)

def swa_prompt(q, k, v, sinks, slopes):
    B, T = q.shape[0], q.shape[1]
    nb = T // ATTN_BLOCK
    qb = q.reshape(B, nb, ATTN_BLOCK, N_KV_HEADS, GROUP, HEAD_DIM)
    kb = k.reshape(B, nb, ATTN_BLOCK, N_KV_HEADS, HEAD_DIM)
    vb = v.reshape(B, nb, ATTN_BLOCK, N_KV_HEADS, HEAD_DIM)
    prev = lambda a: jnp.concatenate([jnp.zeros_like(a[:, :1]), a[:, :-1]], axis=1)
    kband = jnp.concatenate([prev(kb), kb], axis=2)
    vband = jnp.concatenate([prev(vb), vb], axis=2)
    qi = jnp.arange(ATTN_BLOCK)[:, None] + ATTN_BLOCK
    kj = jnp.arange(2 * ATTN_BLOCK)[None, :]
    diff = qi - kj
    blk = jnp.arange(nb)[:, None, None]
    key_ok = (blk * ATTN_BLOCK + kj[None] - ATTN_BLOCK) >= 0
    valid = (((diff >= 0) & (diff <= WINDOW))[None] & key_ok)[:, None, None]
    o = sink_attend(qb, kband, vband, diff, valid, sinks, slopes)
    w = min(WINDOW, T)
    return o.reshape(B, T, ATTN_WIDTH), k[:, T - w:], v[:, T - w:]

def swa_sample(q, k, v, cache_k, cache_v, sinks, slopes):
    T = q.shape[1]
    w_buf = cache_k.shape[1]
    kf = jnp.concatenate([cache_k, k], axis=1)
    vf = jnp.concatenate([cache_v, v], axis=1)
    diff = (jnp.arange(T)[:, None] + w_buf) - jnp.arange(w_buf + T)[None, :]
    valid = (diff >= 0) & (diff <= WINDOW)
    o = sink_attend(q, kf, vf, diff, valid, sinks, slopes)
    return o.reshape(q.shape[0], T, ATTN_WIDTH), kf[:, T:], vf[:, T:]

def causal_mix_matrix(sgu_w):
    mask = jnp.tril(jnp.ones((SGU_CHUNK, SGU_CHUNK), dtype=bool))
    return sgu_w * mask.astype(sgu_w.dtype)

def sgu_prompt(u, v, g, sgu_w, sgu_b):
    B, T, _ = v.shape
    nc = T // SGU_CHUNK
    vn = rmsnorm(v, g).reshape(B, nc, SGU_CHUNK, SGU_GROUPS, SGU_GROUP_DIM)
    mixed = jnp.einsum('gts,bcsgd->bctgd', causal_mix_matrix(sgu_w), vn) + sgu_b.T[None, None, :, :, None]
    return u * mixed.reshape(B, T, SGU_WIDTH)

def sgu_sample(u, v, g, sgu_w, sgu_b):
    Bd, T, _ = v.shape
    vn = rmsnorm(v, g)
    vg = vn.reshape(Bd, T, SGU_GROUPS, SGU_GROUP_DIM)
    w = causal_mix_matrix(sgu_w)[:, :T, :T]
    mixed = jnp.einsum('gts,bsgd->btgd', w, vg) + sgu_b[:, :T].T[None, :, :, None]
    return u * mixed.reshape(Bd, T, SGU_WIDTH), vn

def merge_and_ffn(x, a, b, ga, gb, w_oa, w_ob, w_out, ln2_g, w_up, w_down):
    h = jax.nn.sigmoid(ga) * (a @ w_oa) + jax.nn.sigmoid(gb) * (b @ w_ob)
    x = x + h @ w_out
    xn = rmsnorm(x, ln2_g)
    return x + jnp.square(jax.nn.relu(xn @ w_up)) @ w_down

def setup_inputs(seed: int = 0) -> dict:
    key = jax.random.key(seed)
    ks = jax.random.split(key, 20)
    nrm = lambda k, shape, scale: jax.random.normal(k, shape, jnp.float32) * scale
    gain = lambda k, shape: 1.0 + nrm(k, shape, 0.02)
    cache_shape = (DEPTH, DEC_BATCH, WINDOW, N_KV_HEADS, HEAD_DIM)
    return {
        "x_prompt": nrm(ks[0], (BATCH, SEQ, D_MODEL), 1.0),
        "x_sample": nrm(ks[1], (DEC_BATCH, DEC_SEQ, D_MODEL), 1.0),
        "cache_k_win": nrm(ks[2], cache_shape, 1.0),
        "cache_v_win": nrm(ks[3], cache_shape, 1.0),
        "ln1_g": gain(ks[4], (DEPTH, D_MODEL)),
        "w_in": nrm(ks[5], (DEPTH, D_MODEL, IN_WIDTH), D_MODEL ** -0.5),
        "sgu_norm_g": gain(ks[6], (DEPTH, SGU_WIDTH)),
        "sgu_w": nrm(ks[7], (DEPTH, SGU_GROUPS, SGU_CHUNK, SGU_CHUNK), 0.5 * SGU_CHUNK ** -0.5),
        "sgu_b": 1.0 + nrm(ks[8], (DEPTH, SGU_GROUPS, SGU_CHUNK), 0.1),
        "attn_sinks": nrm(ks[9], (DEPTH, N_HEADS), 1.0),
        "w_oa": nrm(ks[10], (DEPTH, SGU_WIDTH, D_MODEL), SGU_WIDTH ** -0.5),
        "w_ob": nrm(ks[11], (DEPTH, ATTN_WIDTH, D_MODEL), ATTN_WIDTH ** -0.5),
        "w_out": nrm(ks[12], (DEPTH, D_MODEL, D_MODEL), D_MODEL ** -0.5),
        "ln2_g": gain(ks[13], (DEPTH, D_MODEL)),
        "w_up": nrm(ks[14], (DEPTH, D_MODEL, D_FF), D_MODEL ** -0.5),
        "w_down": nrm(ks[15], (DEPTH, D_FF, D_MODEL), D_FF ** -0.5),
        "lnf_g": gain(ks[16], (D_MODEL,)),
    }

def reference(x_prompt, x_sample, cache_k_win, cache_v_win, ln1_g, w_in, sgu_norm_g, sgu_w, sgu_b,
              attn_sinks, w_oa, w_ob, w_out, ln2_g, w_up, w_down, lnf_g):
    slopes = alibi_slopes().astype(jnp.float32)
    xp, xs = x_prompt, x_sample
    kp_l, vp_l, ks_l, vs_l, sv_l = [], [], [], [], []
    for l in range(DEPTH):
        u, v, q, k, va, ga, gb = in_proj(xp, ln1_g[l], w_in[l])
        a = sgu_prompt(u, v, sgu_norm_g[l], sgu_w[l], sgu_b[l])
        b, kw, vw = swa_prompt(q, k, va, attn_sinks[l], slopes)
        xp = merge_and_ffn(xp, a, b, ga, gb, w_oa[l], w_ob[l], w_out[l], ln2_g[l], w_up[l], w_down[l])
        kp_l.append(kw)
        vp_l.append(vw)
        u, v, q, k, va, ga, gb = in_proj(xs, ln1_g[l], w_in[l])
        a, vrows = sgu_sample(u, v, sgu_norm_g[l], sgu_w[l], sgu_b[l])
        b, kw, vw = swa_sample(q, k, va, cache_k_win[l], cache_v_win[l], attn_sinks[l], slopes)
        xs = merge_and_ffn(xs, a, b, ga, gb, w_oa[l], w_ob[l], w_out[l], ln2_g[l], w_up[l], w_down[l])
        ks_l.append(kw)
        vs_l.append(vw)
        sv_l.append(vrows)
    y_prompt = rmsnorm(xp, lnf_g)
    y_sample = rmsnorm(xs, lnf_g)
    new_k_win_prompt = jnp.stack(kp_l)
    new_v_win_prompt = jnp.stack(vp_l)
    new_k_win_sample = jnp.stack(ks_l)
    new_v_win_sample = jnp.stack(vs_l)
    new_sgu_v_sample = jnp.stack(sv_l)
    return (y_prompt, y_sample, new_k_win_prompt, new_v_win_prompt, new_k_win_sample, new_v_win_sample, new_sgu_v_sample)


_drawn_inputs = setup_inputs


def setup_inputs(seed=0):
    import zlib

    import numpy as np

    out = dict(_drawn_inputs(seed))
    spreads = {}
    factors = {'ln1_g': 2.717, 'sgu_norm_g': 19.523, 'ln2_g': 3.099, 'lnf_g': 23.461, 'attn_sinks': 5.943}
    for name, (base, spread) in spreads.items():
        noise = np.random.default_rng([zlib.crc32(name.encode()), seed]).standard_normal(out[name].shape)
        drawn = base * np.exp(spread * noise) if base else spread * noise
        out[name] = __import__('jax').numpy.asarray(drawn.astype(out[name].dtype))
    for name, factor in factors.items():
        out[name] = (out[name] * factor).astype(out[name].dtype)
    return out
```

```python
from contextlib import ExitStack

import concourse.bass as bass
from concourse import mybir
from concourse.alu_op_type import AluOpType as ALU

F32 = mybir.dt.float32
F32R = mybir.dt.float32r
ACT = mybir.ActivationFunctionType
ds = bass.ds


class Chain:

    def __init__(self, eng, sem):
        self.eng, self.sem, self.n, self.local, self.outer = eng, sem, 0, 0, []

    def link(self, instruction):
        instruction.then_inc(self.sem, 1)
        self.local += 1
        self.eng.wait_ge(self.sem, self.n + self.local)

    def enter(self, i, per):
        self.outer.append((self.n + self.local, per))
        self.n, self.local = self.n + self.local + i * per, 0

    def leave(self, turns):
        before, per = self.outer.pop()
        assert self.local == per, self.local
        self.n, self.local = before + turns * per, 0


def build_trunk(nc, x_prompt, x_sample, cache_k, cache_v, ln1_g, w_in, sgu_norm_g, sgu_w, sgu_b,
                sinks, w_oa, w_ob, w_out, ln2_g, w_up, w_down, lnf_g,
                y_prompt, y_sample, k_win_p, v_win_p, k_win_s, v_win_s, sgu_v_s):
    P = 128
    SEQ, D = x_prompt.shape[1], x_prompt.shape[2]
    NB = x_sample.shape[0]
    T = SEQ + NB
    NT = 3
    TN = T // NT
    KT = D // P
    NBLK = SEQ // P
    NTOK = NBLK + 1
    W, NG, HD = cache_k.shape[2], cache_k.shape[3], cache_k.shape[4]
    H = sinks.shape[1]
    HPG = H // NG
    GS = sgu_w.shape[1]
    NC = w_up.shape[2] // D
    EPS = 1e-6
    SCALE = float(HD) ** -0.5
    ROWS = [P] * NBLK + [NB]
    assert T == NT * TN and TN <= 512 and W == P and HD == 64 and HPG == 4 and GS == KT and NB * H == P

    OU, OV, OQ = 0, D, 2 * D
    OK = OQ + H * HD
    OVA = OK + NG * HD
    OGA = OVA + NG * HD
    OGB = OGA + D
    w_in, w_oa, w_ob, w_out = w_in[0], w_oa[0], w_ob[0], w_out[0]
    w_up, w_down = w_up[0], w_down[0]

    RB = [(6, NBLK, NTOK), (7, 0, 4), (6, 4, NBLK)]

    JA = 0
    JB = JA + 3 * NG
    JC = JB + 2 * KT
    JD = JC + KT
    JE = JD + KT
    JF = JE + 2 * KT
    JG = JF + KT
    JN = JG + NC * 2 * KT
    NU = NG * NBLK

    with ExitStack() as ctx:
        at = [(nc.sbuf_base + 31) // 32 * 32]

        def region(nbytes):
            start = at[0]
            at[0] += (nbytes + 31) // 32 * 32
            assert at[0] <= nc.sbuf_usable_end, at[0]
            return start

        def place(name, shape, dt, offset):
            return nc.alloc_sbuf_tensor_at(name, shape, dt, offset=offset)

        def sb(name, shape, dt=F32):
            n = 4
            for s in shape[1:]:
                n *= s
            return place(name, shape, dt, region(n))

        ACTB = KT * T * 4
        r_0, r_0b, r_1, r_2, r_3 = (region(ACTB) for _ in range(5))
        xn_hi = place("xn_hi", [P, KT, T], F32R, r_0)
        xn_lo = place("xn_lo", [P, KT, T], F32R, r_0b)
        h_hi = place("h_hi", [P, KT, T], F32R, r_0)
        h_lo = place("h_lo", [P, KT, T], F32R, r_0b)
        r_hi = place("r_hi", [P, KT, T], F32R, r_0)
        r_lo = place("r_lo", [P, KT, T], F32R, r_0b)
        x_stage = place("x_stage", [P, NTOK, D], F32, r_1)
        b_hi = place("b_hi", [P, KT, T], F32R, r_1)
        mix = place("mix", [P, KT, T], F32, r_1)
        a_hi = place("a_hi", [P, KT, T], F32R, r_1)
        res = place("res", [P, KT, T], F32, r_1)
        b_lo = place("b_lo", [P, KT, T], F32R, r_2)
        a_lo = place("a_lo", [P, KT, T], F32R, r_2)
        xf_hi = place("xf_hi", [P, KT, T], F32R, r_2)
        x_again = place("x_again", [P, NBLK, D], F32, r_2)
        sgu_raw = place("sgu_raw", [P, GS, P], F32, r_2)
        vn = place("vn", [P, 2, D], F32, r_2 + 4 * D)
        gv_row = place("gv_row", [NB, D], F32, r_2 + 12 * D)
        vs_out = place("vs_out", [NB, D], F32, r_2 + 16 * D)
        wt_dec = place("wt_dec", [NB, GS, NB], F32, r_2 + 20 * D)
        xg = place("xg", [P, 2, KT, P], F32, r_3)
        q_st = place("q_st", [P, HPG, T], F32R, r_3)
        ck = place("ck", [P, NB, NG * HD], F32, r_3)
        cv = place("cv", [P, NB, NG * HD], F32, r_3 + NB * NG * HD * 4)
        o = r_3 + HPG * T * 4
        abias = place("abias", [P, HPG, 2 * P], F32, o)
        o += HPG * 2 * P * 4
        SW = 2 * P + 1
        prob = place("prob", [P, 2, HPG, SW], F32, o)
        kv_t = place("kv_t", [P, T], F32, o)
        st_sb = place("st_sb", [P, P], F32, o)
        prod_t = place("prod_t", [HD, NB, H], F32, o + 512)
        dbias = place("dbias", [P, W + 1], F32, o + 1024)
        dprob = place("dprob", [P, W + 2], F32, o + 1024 + 544)
        dp_t = place("dp_t", [P, NB, H], F32, o + 2624)
        dself = place("dself", [P, P], F32, o + 3136)
        d_o = place("d_o", [P, NB, H], F32, o + 3648)
        o += 2 * HPG * SW * 4
        v_dup = place("v_dup", [P, NBLK, 2 * HD], F32, o)
        assert o + NBLK * 2 * HD * 4 <= r_3 + ACTB
        h_f = place("h_f", [P, KT, T], F32, r_3)
        xf_lo = place("xf_lo", [P, KT, T], F32R, r_3)
        y_t = place("y_t", [P, 2, D], F32, r_3)

        raw = sb("raw", [P, 2, KT, P])
        w_hi = sb("w_hi", [P, 2, KT, P], F32R)
        w_lo = sb("w_lo", [P, 2, KT, P], F32R)

        ident = sb("ident", [P, P])
        ones = sb("ones", [P, P])
        g1, g2, gv = sb("g1", [P, KT]), sb("g2", [P, KT]), sb("gv", [P, KT])
        ssq, var, rstd = sb("ssq", [P, NTOK]), sb("var", [P, NTOK]), sb("rstd", [P, NTOK])
        mhalf = sb("mhalf", [P, NTOK])
        slopes, nsink = sb("slopes", [P, H]), sb("nsink", [P, H])
        nsink_g = sb("nsink_g", [P, HPG])
        slope_row, nsink_row = sb("slope_row", [P, 1]), sb("nsink_row", [P, 1])
        nmax, den, rden = (sb(n, [P, 2, HPG]) for n in ("nmax", "den", "rden"))
        dstat = sb("dstat", [P, 4])
        q_dec = sb("q_dec", [HD, NB, H])
        k_dec, v_dec = sb("k_dec", [HD, NG, NB]), sb("v_dec", [HD, NG, NB])
        wt00 = sb("wt00", [NB, GS])

        r_s = region(4 * D + 4 * D + 3 * T * 4)
        dist8 = place("dist8", [P, 2 * P], F32, r_s)
        k_hi = place("k_hi", [P, T], F32R, r_s + 1024)
        k_lo = place("k_lo", [P, T], F32R, r_s + 1024 + 4 * T)
        p_t = place("p_t", [P, 2, 2, HPG, P], F32, r_s + 1024 + 8 * T)
        ck_t = place("ck_t", [HD, 2, NG, P], F32, r_s + 1024 + 8 * T)
        kv_tail = place("kv_tail", [P, 2, 2 * HD], F32, r_s + 1024 + 8 * T + 8192)
        wt = place("wt", [P, GS, P], F32, r_s)
        bb = place("bb", [P, GS, P], F32, r_s + 4 * D)
        rstd_b = place("rstd_b", [P, T], F32, r_s)
        gf_row = place("gf_row", [P, D], F32, r_s + 8 * D + 8 * T)
        x_dec = place("x_dec", [NB, D], F32, r_s)
        tmp = place("tmp", [P, 2, T], F32, r_s + 8 * D)
        sq_sum = place("sq_sum", [P, T], F32, r_s + 8 * D + 8 * T)

        ps = ctx.enter_context(nc.psum_tensor("ps", [P, 8, 512], F32))

        def pset(s, rows=slice(0, P)):
            return ps[rows, 3 * s:3 * s + 3, 0:TN]

        def by3(ap):
            return ap.rearrange("p (b t) -> p b t", b=NT)

        def toks(t):
            return slice(t * P, t * P + ROWS[t])

        def sem(name):
            return ctx.enter_context(nc.semaphore(name))

        w_loaded = [sem("w_loaded0"), sem("w_loaded1")]
        w_hi_ready, w_split = sem("w_hi_ready"), sem("w_split")
        job_done = sem("job_done")
        set_free = [sem("set_free0"), sem("set_free1")]
        small_in = sem("small_in")
        const_ready = sem("const_ready")
        chain_a, chain_v, chain_p = sem("chain_a"), sem("chain_v"), sem("chain_p")
        x_in = [sem(f"x_in{t}") for t in range(NTOK)]
        sq_done, rstd_done, xs_done, xt_done = sem("sq_done"), sem("rstd_done"), sem("xs_done"), sem("xt_done")
        xg_done, xhi_done, xn_done = sem("xg_done"), sem("xhi_done"), sem("xn_done")
        abias_ready = sem("abias_ready")
        kv_t_ready, k_hi_ready = sem("kv_t_ready"), sem("k_hi_ready")
        q_hi_ready = sem("q_hi_ready")
        kv_turned, v_moved, tail_ready, tail_out = sem("kv_turned"), sem("v_moved"), sem("tail_ready"), sem("tail_out")
        scores_ready, scores_masked = sem("scores_ready"), sem("scores_masked")
        exp_done, rden_done, probs_ready, probs_turned = sem("exp_done"), sem("rden_done"), sem("probs_ready"), sem("probs_turned")
        pt_a, pt_v = sem("pt_a"), sem("pt_v")
        pv_done = sem("pv_done")
        o_hi, o_lo = sem("o_hi"), sem("o_lo")
        cache_in, dk_turned, dk_moved, dst_ready = sem("cache_in"), sem("dk_turned"), sem("dk_moved"), sem("dst_ready")
        dst_done = sem("dst_done")
        db_hi = sem("db_hi")
        dst_moved, dprod_ready, ds_ready, dmasked, dexp = sem("dst_moved"), sem("dprod_ready"), sem("ds_ready"), sem("dmasked"), sem("dexp")
        dprobs, dp_turned, dp_moved, dpv_done, do_ready, db_ready = (sem(n) for n in ("dprobs", "dp_turned", "dp_moved", "dpv_done", "do_ready", "db_ready"))
        dbias_ready = sem("dbias_ready")
        h_ready, nsink_ready = sem("h_ready"), sem("nsink_ready")
        sgu_in, sgu_masked, wt_turned, wt_ready = sem("sgu_in"), sem("sgu_masked"), sem("wt_turned"), sem("wt_ready")
        vt_turned, v_sq, v_sq_added, v_ss, v_var, v_rstd, vn_ready, mixed, scaled, mix_ready = (sem(n) for n in ("vt_turned", "v_sq", "v_sq_added", "v_ss", "v_var", "v_rstd", "vn_ready", "mixed", "scaled", "mix_ready"))
        vs_ready, vs_stored = sem("vs_ready"), sem("vs_stored")
        u_ready, a_ready, a_hi_ready, a_lo_ready = sem("u_ready"), sem("a_ready"), sem("a_hi_ready"), sem("a_lo_ready")
        h_hi_ready, h_split = sem("h_hi_ready"), sem("h_split")
        xr_turned, xr_moved = sem("xr_turned"), [sem("xr_moved0"), sem("xr_moved1")]
        sq_ready, sq_added = sem("sq_ready"), sem("sq_added")
        ss_ready, var_ready, rs_ready, rb_ready, rb_moved = (sem(n) for n in ("ss_ready", "var_ready", "rs_ready", "rb_ready", "rb_moved"))
        xf_hi_ready, xf_split = sem("xf_hi_ready"), sem("xf_split")
        r_ready, r_hi_ready, r_split = sem("r_ready"), sem("r_hi_ready"), sem("r_split")
        y_turned, y_sq, y_rstd, y_ready = (sem(n) for n in ("y_turned", "y_sq", "y_rstd", "y_ready"))
        y_stored = [sem("y_stored0"), sem("y_stored1")]
        gf_in = sem("gf_in")
        win_stored = sem("win_stored")
        block = ctx.enter_context(nc.Block())

        @block.sync
        def _(sp):
            for t in range(NBLK):
                sp.dma_start(x_stage[:, t, :], x_prompt[0, t * P:(t + 1) * P, :]).then_inc(x_in[t], 16)

            def load(j, s, two):
                sp.wait_ge(w_split, j + 1)
                for dst, src in two:
                    sp.dma_start(dst, src).then_inc(w_loaded[s], 16)

            def load_block(j, s, w, row, col):
                halves = w[ds(row, D), ds(col, P)].rearrange("(two k p) n -> two p k n", two=2, p=P)
                load(j, s, [(raw[:, s, h * KT // 2:(h + 1) * KT // 2, :], halves[h]) for h in (1, 0)])

            with sp.Fori(0, NG // 2) as gp:
                for g2_ in range(2):
                    j, g, s = gp * 6 + 3 * g2_, gp * 2 + g2_, g2_ % 2
                    load(j, s, [(raw[:, s, :, half * HD:(half + 1) * HD],
                                 w_in[:, ds(g * HD + col, HD)].rearrange("(k p) n -> p k n", p=P))
                                for half, col in ((0, OK), (1, OVA))])
                    load_block(j + 1, 1 - s, w_in, 0, g * 2 * P + OQ)
                    load_block(j + 2, s, w_in, 0, g * 2 * P + P + OQ)
            with sp.Fori(JB // 2, JB // 2 + KT) as h:
                load_block(h * 2, 0, w_in, 0, (h - JB // 2) * P + OGB)
                load_block(h * 2 + 1, 1, w_ob, 0, (h - JB // 2) * P)
            for j0, col in ((JC, OV), (JD, OU)):
                with sp.Fori(0, KT // 2) as i:
                    for s in range(2):
                        load_block(i * 2 + j0 + s, s, w_in, 0, i * 2 * P + s * P + col)
            with sp.Fori(JE // 2, JE // 2 + KT) as h:
                load_block(h * 2, 0, w_in, 0, (h - JE // 2) * P + OGA)
                load_block(h * 2 + 1, 1, w_oa, 0, (h - JE // 2) * P)
            with sp.Fori(0, KT // 2) as i:
                for s in range(2):
                    load_block(i * 2 + JF + s, s, w_out, 0, i * 2 * P + s * P)
            with sp.Fori(0, NC) as c:
                with sp.Fori(0, KT // 2) as i:
                    for s in range(2):
                        load_block(c * 2 * KT + i * 2 + JG + s, s, w_up, 0, c * D + i * 2 * P + s * P)
                with sp.Fori(0, KT // 2) as i:
                    for s in range(2):
                        load_block(c * 2 * KT + i * 2 + JG + KT + s, s, w_down, c * D, i * 2 * P + s * P)
            for t in range(NTOK):
                sp.wait_ge(y_ready, t + 1)
                dst = y_prompt[0, t * P:(t + 1) * P, :] if t < NBLK else y_sample[:, 0, :]
                sp.dma_start(dst, y_t[0:ROWS[t], t % 2, :]).then_inc(y_stored[t % 2], 16)
            for s in range(2):
                sp.wait_ge(y_stored[s], 16 * ((NTOK + 1 - s) // 2))
            sp.wait_ge(vs_stored, 16)
            sp.wait_ge(win_stored, 32)
            sp.wait_ge(tail_out, 64 * NG + 64)

        @block.gpsimd
        def _(pool):
            chain = Chain(pool, chain_p)
            pool.sem_inc(w_split, 2)
            pool.sem_inc(job_done, 1)
            pool.sem_inc(set_free[0], 1)
            pool.sem_inc(set_free[1], 1)
            pool.sem_inc(scores_masked, 2)
            pool.sem_inc(probs_turned, 2)
            pool.sem_inc(pt_a, 1)
            pool.sem_inc(pt_v, 1)
            pool.sem_inc(pv_done, 2)
            pool.sem_inc(o_lo, 1)
            pool.sem_inc(tail_out, 64)
            pool.sem_inc(a_lo_ready, 2)
            pool.sem_inc(r_split, 2)
            pool.sem_inc(sq_added, 2)
            pool.sem_inc(v_sq_added, 2)
            pool.sem_inc(h_ready, 1)
            nc.gpsimd.memset(mhalf[:, :], -0.5)
            chain.link(nc.gpsimd.memset(ident[:, :], 0.0))
            nc.gpsimd.affine_select(out=ident[:, :], in_=ident[:, :], compare_op=ALU.not_equal, fill=1.0,
                                    base=0, pattern=[[-1, P]], channel_multiplier=1).then_inc(const_ready, 1)

            def low(t):
                r = ROWS[t]
                pool.wait_ge(xhi_done, t + 1)
                nc.gpsimd.tensor_tensor(xn_lo[:, :, toks(t)], xg[:, t % 2, :, 0:r],
                                        xn_hi[:, :, toks(t)].bitcast(F32), ALU.subtract).then_inc(xn_done, 1)

            for t in range(NTOK):
                r = ROWS[t]
                pool.wait_ge(sq_done, t + 1)
                chain.link(nc.gpsimd.tensor_scalar(var[0:r, t:t + 1], ssq[0:r, t:t + 1], 1.0 / D, EPS,
                                                   ALU.mult, ALU.add))
                nc.gpsimd.tensor_tensor(rstd[0:r, t:t + 1], var[0:r, t:t + 1], mhalf[0:r, 0:1],
                                        ALU.pow).then_inc(rstd_done, 1)
                if t >= 2:
                    low(t - 2)
            low(NTOK - 2)
            low(NTOK - 1)

            for h in range(H):
                nc.gpsimd.memset(slopes[:, h:h + 1], 2.0 ** (-8.0 * (h + 1) / H))
            nc.gpsimd.memset(ones[:, :], 1.0)
            chain.link(nc.gpsimd.iota(dist8[:, :], pattern=[[8, 2 * P]], base=-8 * P, channel_multiplier=-8,
                                      allow_small_or_imprecise_dtypes=True))
            chain.link(nc.gpsimd.affine_select(out=dist8[:, :], in_=dist8[:, :], compare_op=ALU.is_ge,
                                               fill=-1e34, base=P, pattern=[[-1, 2 * P]], channel_multiplier=1))
            chain.link(nc.gpsimd.affine_select(out=dist8[:, :], in_=dist8[:, :], compare_op=ALU.is_ge,
                                               fill=-1e34, base=0, pattern=[[1, 2 * P]], channel_multiplier=-1))
            nc.gpsimd.memset(sq_sum[:, 0:1], 0.0).then_inc(const_ready, 1)

            def unit(u, slot, b):
                lo = P if b == 0 else 0
                pool.wait_ge(rden_done, u + 1)
                p = prob[:, slot, :, lo:2 * P]
                nc.gpsimd.tensor_tensor(p, p, rden[:, slot, :].unsqueeze(2).to_broadcast([P, HPG, 2 * P - lo]),
                                        ALU.mult).then_inc(probs_ready, 1)

            with pool.Fori(0, NG // 2) as gp:
                for g2_ in range(2):
                    g = gp * 2 + g2_
                    pool.wait_ge(scores_masked, g * NBLK + 2)
                    pool.wait_ge(nsink_ready, 1)
                    nc.gpsimd.tensor_copy(nsink_g[:, :], nsink[:, ds(g * HPG, HPG)])
                    nc.gpsimd.tensor_tensor(
                        abias[:, :, :], dist8[:, :].unsqueeze(1).to_broadcast([P, HPG, 2 * P]),
                        slopes[:, ds(g * HPG, HPG)].unsqueeze(2).to_broadcast([P, HPG, 2 * P]),
                        ALU.mult).then_inc(abias_ready, 1)
                    for b in range(NBLK):
                        unit(g * NBLK + b, b % 2, b)

            pool.wait_ge(pv_done, NU + 2)
            nc.gpsimd.iota(dbias[:, :], pattern=[[8, W + 1]], base=-8 * W, channel_multiplier=0,
                           allow_small_or_imprecise_dtypes=True).then_inc(dbias_ready, 1)

            def add_squares(ready, added):
                with pool.Fori(0, KT // 2) as i:
                    for s in range(2):
                        pool.wait_ge(ready, i * 2 + s + 1)
                        pool.wait_ge(added, i * 2 + s + 2)
                        nc.gpsimd.tensor_tensor(sq_sum[:, :], sq_sum[:, :], tmp[:, s, :], ALU.add).then_inc(added, 1)

            def rstd_of_all(done):
                nc.gpsimd.tensor_tensor(rstd[:, 0:NBLK], var[:, 0:NBLK], mhalf[:, 0:NBLK], ALU.pow)
                nc.gpsimd.tensor_tensor(rstd[0:NB, NBLK:], var[0:NB, NBLK:], mhalf[0:NB, NBLK:],
                                        ALU.pow).then_inc(done, 1)

            def add_bias(t):
                r = ROWS[t]
                pool.wait_ge(scaled, t + 1)
                m = mix[:, :, toks(t)]
                bias = bb[:, :, :] if t < NBLK else bb[:, :, 0:1].to_broadcast([P, GS, r])
                nc.gpsimd.tensor_tensor(m, m, bias, ALU.add).then_inc(mix_ready, 1)

            pool.wait_ge(sgu_in, 64)
            nc.gpsimd.affine_select(out=sgu_raw[:, :, :], in_=sgu_raw[:, :, :], compare_op=ALU.is_ge, fill=0.0,
                                    base=0, pattern=[[0, GS], [-1, P]], channel_multiplier=1).then_inc(sgu_masked, 1)
            pool.wait_ge(tail_out, 64 * NG + 64)
            chain.link(nc.gpsimd.memset(sq_sum[:, :], 0.0))
            add_squares(v_sq, v_sq_added)
            pool.wait_ge(v_var, 1)
            rstd_of_all(v_rstd)
            for t in range(NTOK):
                add_bias(t)

            with pool.Fori(0, KT) as n:
                pool.wait_ge(set_free[1], n + JE // 2 + 2)
                hn = h_f[:, ds(n, 1), :].rearrange("p a t -> p (a t)")
                nc.gpsimd.tensor_tensor(hn, hn, tmp[:, 1, :], ALU.add).then_inc(h_ready, 1)

            chain.link(nc.gpsimd.memset(sq_sum[:, :], 0.0))
            add_squares(sq_ready, sq_added)
            pool.wait_ge(var_ready, 1)
            rstd_of_all(rs_ready)
            for t in range(NTOK):
                r = ROWS[t]
                pool.wait_ge(y_sq, t + 1)
                chain.link(nc.gpsimd.tensor_scalar(var[0:r, t:t + 1], ssq[0:r, t:t + 1], 1.0 / D, EPS,
                                                   ALU.mult, ALU.add))
                nc.gpsimd.tensor_tensor(rstd[0:r, t:t + 1], var[0:r, t:t + 1], mhalf[0:r, 0:1],
                                        ALU.pow).then_inc(y_rstd, 1)

        @block.scalar
        def _(act):
            def copy(dst, src):
                return nc.scalar.activation(dst, src, ACT.Copy)

            def copy_scaled(dst, src, scale):
                return nc.scalar.activation(dst, src, ACT.Copy, scale=scale)

            act.dma_start(x_stage[0:NB, NBLK, :], x_sample[:, 0, :]).then_inc(x_in[NBLK], 16)
            with nc.allow_non_contiguous_dma(reason="gains to partitions, 4 KB each"):
                for dst, src in ((g1, ln1_g[0]), (g2, ln2_g[0]), (gv, sgu_norm_g[0])):
                    act.dma_start(dst[:, :], src.rearrange("(k p) -> p k", p=P)).then_inc(small_in, 16)
            act.dma_start(nsink[:, :], sinks.to_broadcast([P, H])).then_inc(small_in, 16)
            for dst, src in ((k_win_s, cache_k), (v_win_s, cache_v)):
                act.dma_start(dst[0, :, 0:W - 1].rearrange("b t g d -> b (t g d)"),
                              src[0, :, 1:W].rearrange("b t g d -> b (t g d)")).then_inc(win_stored, 16)

            def square(out, src, t):
                r = ROWS[t]
                return nc.scalar.activation(out, src, ACT.Square, accum_out=ssq[0:r, t:t + 1])

            def high(t):
                r = ROWS[t]
                act.wait_ge(xg_done, t + 1)
                copy(xn_hi[:, :, toks(t)], xg[:, t % 2, :, 0:r]).then_inc(xhi_done, 1)

            for t in range(NTOK):
                r = ROWS[t]
                act.wait_ge(x_in[t], 16)
                if t >= 1:
                    act.wait_ge(sq_done, t)
                square(ps[0:r, 6:8, :], x_stage[0:r, t, :].rearrange("p (a b) -> p a b", a=2), t).then_inc(sq_done, 1)
                if t >= 2:
                    high(t - 2)
            high(NTOK - 2)
            high(NTOK - 1)

            def split_hi(j, h, s):
                act.wait_ge(w_loaded[s], h * 32 + 32)
                act.wait_ge(job_done, j + 0)
                copy(w_hi[:, s], raw[:, s]).then_inc(w_hi_ready, 1)

            act.wait_ge(w_loaded[0], 32)
            copy(w_hi[:, 0], raw[:, 0]).then_inc(w_hi_ready, 1)

            def exps(u, slot, b):
                lo = P if b == 0 else 0
                act.wait_ge(scores_masked, u + 3)
                for h in range(HPG):
                    s_ = prob[:, slot, h, lo:SW]
                    last = nc.scalar.activation(s_, s_, ACT.Exp, scale=-1.0, bias=nmax[:, slot, h:h + 1],
                                                accum_out=den[:, slot, h:h + 1])
                last.then_inc(exp_done, 1)

            def move_pt(u, slot, b):
                act.wait_ge(probs_turned, u + 3)
                act.wait_ge(pv_done, u + 1)
                copy(p_t[:, slot, 1, :, :], ps[:, 5, :].rearrange("p (h q) -> p h q", h=HPG)).then_inc(pt_a, 1)

            def out_hi(u, g, b):
                act.wait_ge(pv_done, u + 3)
                for par in range(2):
                    rows = slice(par * HD, (par + 1) * HD)
                    src = ps[rows, 6, :].rearrange("p (t r q) -> p r t q", t=2, r=2)[:, par]
                    last = copy(b_hi[rows, ds(g * 2, 2), b * P:(b + 1) * P], src)
                last.then_inc(o_hi, 1)

            def q_high(j, s, pair):
                act.wait_ge(job_done, j + 2)
                copy(by3(q_st[0:HD, 2 * pair, :]), pset(s, slice(0, HD)))
                copy(by3(q_st[0:HD, 2 * pair + 1, :]), pset(s, slice(HD, P))).then_inc(q_hi_ready, 1)

            with act.Fori(0, NG // 2) as gp:
                for g2_ in range(2):
                    g, u0 = gp * 2 + g2_, gp * 2 * NBLK + g2_ * NBLK
                    L = 3 * g2_

                    def job(n):
                        return gp * 6 + n, gp * 3 + n // 2, n % 2

                    split_hi(*job(L + 1))
                    j, _, s = job(L)
                    act.wait_ge(job_done, j + 2)
                    copy(by3(kv_t[:, :]), pset(s)).then_inc(kv_t_ready, 1)
                    copy(by3(k_hi[0:HD, :]), pset(s, slice(0, HD)))
                    copy(by3(k_hi[HD:P, :]), pset(s, slice(0, HD))).then_inc(k_hi_ready, 1)
                    split_hi(*job(L + 2))
                    q_high(j + 1, 1 - s, 0)
                    split_hi(*job(L + 3))
                    q_high(j + 2, s, 1)
                    exps(u0, 0, 0)
                    exps(u0 + 1, 1, 1)
                    act.wait_ge(tail_ready, g * 2 + 2)
                    for kv, (wp, ws) in enumerate(((k_win_p, k_win_s), (v_win_p, v_win_s))):
                        act.dma_start(ws[0, :, W - 1].rearrange("b g d -> b (g d)")[:, ds(g * HD, HD)],
                                     kv_tail[0:NB, 1, kv * HD:(kv + 1) * HD]).then_inc(tail_out, 16)
                        act.dma_start(wp[0, 0].rearrange("t g d -> t (g d)")[:, ds(g * HD, HD)],
                                     kv_tail[:, 0, kv * HD:(kv + 1) * HD]).then_inc(tail_out, 16)
                    for b in range(NBLK):
                        move_pt(u0 + b, b % 2, b)
                        if b >= 1:
                            out_hi(u0 + b - 1, g, b - 1)
                        if b + 2 < NBLK:
                            exps(u0 + b + 2, b % 2, b + 2)
                    out_hi(u0 + NBLK - 1, g, NBLK - 1)

            act.wait_ge(pv_done, NU + 2)
            for dst, src in ((ck, cache_k), (cv, cache_v)):
                act.dma_start(dst[:, :, :], src[0].rearrange("b w g d -> w b (g d)")).then_inc(cache_in, 16)
            for b in range(NB):
                act.wait_ge(dk_turned, b + 1)
                if b >= 2:
                    act.wait_ge(dst_done, b - 1)
                copy(ck_t[:, b % 2, :, :], ps[0:HD, 6 + b % 2, :].rearrange("p (g w) -> p g w", g=NG)).then_inc(dk_moved, 1)
            act.wait_ge(dmasked, 1)
            nc.scalar.activation(dprob[:, :], dprob[:, :], ACT.Exp, scale=-1.0, bias=dstat[:, 0:1],
                                 accum_out=dstat[:, 1:2]).then_inc(dexp, 1)
            act.wait_ge(do_ready, 1)
            for par in range(2):
                rows = slice(par * HD, (par + 1) * HD)
                last = copy(b_hi[rows, :, SEQ:T], d_o[rows].rearrange("p b (t r) -> p r t b", r=2)[:, par])
            last.then_inc(db_hi, 1)

            def gates(j0):
                with act.Fori(0, KT) as n:
                    j = n * 2 + j0
                    split_hi(j + 1, n + j0 // 2, 1)
                    act.wait_ge(job_done, j + 2)
                    act.wait_ge(set_free[1], n + j0 // 2 + 1)
                    nc.scalar.activation(by3(tmp[:, 0, :]), pset(0), ACT.Sigmoid).then_inc(set_free[0], 1)
                    split_hi(j + 2, n + j0 // 2 + 1, 0)

            gates(JB)

            act.wait_ge(job_done, JC + 1)
            act.dma_start(sgu_raw[:, :, :], sgu_w[0].rearrange("g t s -> t g s")).then_inc(sgu_in, 16)
            act.dma_start(bb[:, :, :].rearrange("p g t -> p (g t)"),
                          sgu_b.rearrange("a g t -> a (g t)").to_broadcast([P, GS * P])).then_inc(sgu_in, 16)
            act.dma_start(gv_row[:, :], sgu_norm_g.to_broadcast([NB, D])).then_inc(sgu_in, 16)
            with nc.allow_non_contiguous_dma(reason="one number of each group"):
                act.dma_start(wt00[:, :], sgu_w[0, :, 0, 0:1].rearrange("g s -> s g").to_broadcast([NB, GS])).then_inc(sgu_in, 16)
            with act.Fori(0, KT // 2) as i:
                for s in range(2):
                    j = i * 2 + JC + s
                    split_hi(j + 1, i + (JC + s + 1) // 2, 1 - s)
                    act.wait_ge(job_done, j + 2)
                    nc.scalar.activation(by3(mix[:, ds(i * 2 + s, 1), :].rearrange("p a t -> p (a t)")), pset(s),
                                         ACT.Gelu_apprx_tanh).then_inc(set_free[s], 1)
            act.wait_ge(v_rstd, 1)
            for t in range(NTOK):
                r, bank = ROWS[t], 2 * (t % 2)
                act.wait_ge(vt_turned, t + 1)
                if t >= 2:
                    act.wait_ge(mixed, t - 1)
                nc.scalar.activation(vn[0:r, t % 2, :].rearrange("p (a b) -> p a b", a=2), ps[0:r, bank:bank + 2, :],
                                     ACT.Copy, scale=rstd[0:r, t:t + 1]).then_inc(vn_ready, 1)
            act.wait_ge(vs_ready, 1)
            act.dma_start(sgu_v_s[0, :, 0, :], vs_out[:, :]).then_inc(vs_stored, 16)
            with act.Fori(0, KT // 2) as i:
                for s in range(2):
                    j, n = i * 2 + JD + s, i * 2 + s
                    split_hi(j + 1, i + (JD + s + 1) // 2, 1 - s)
                    act.wait_ge(job_done, j + 2)
                    act.wait_ge(a_lo_ready, n + 1)
                    nc.scalar.activation(by3(tmp[:, s, :]), pset(s), ACT.Gelu_apprx_tanh).then_inc(set_free[s], 1)
                    act.wait_ge(a_ready, n + 1)
                    copy(a_hi[:, ds(n, 1), :].rearrange("p a t -> p (a t)"), tmp[:, s, :]).then_inc(a_hi_ready, 1)
            gates(JE)
            act.wait_ge(job_done, JF + 1)
            for t in range(NBLK):
                act.dma_start(x_again[:, t, :], x_prompt[0, t * P:(t + 1) * P, :]).then_inc(x_in[t], 16)
            act.dma_start(x_dec[:, :], x_sample[:, 0, :]).then_inc(x_in[NBLK], 16)
            for n in range(KT):
                act.wait_ge(h_ready, n + 2)
                copy(h_hi[:, n, :], h_f[:, n, :]).then_inc(h_hi_ready, 1)
            for t in range(0, NTOK, 2):
                r, bank = ROWS[t], 2 * (t % 3)
                act.wait_ge(xr_turned, t + 1)
                copy(res[:, :, toks(t)], ps[:, bank:bank + 2, :].rearrange("p a (k q) -> p (a k) q", q=P)[:, :, 0:r]).then_inc(xr_moved[0], 1)
            with act.Fori(0, KT // 2) as i:
                for s in range(2):
                    j = i * 2 + JF + s
                    split_hi(j + 1, i + (JF + s + 1) // 2, 1 - s)
                    act.wait_ge(set_free[s], i + JF // 2 + 2)
                    act.wait_ge(sq_added, i * 2 + s + 1)
                    copy_scaled(xf_hi[:, ds(i * 2 + s, 1), :].rearrange("p a t -> p (a t)"),
                                res[:, ds(i * 2 + s, 1), :].rearrange("p a t -> p (a t)"),
                                g2[:, ds(i * 2 + s, 1)]).then_inc(xf_hi_ready, 1)
                    nc.scalar.activation(tmp[:, s, :], res[:, ds(i * 2 + s, 1), :].rearrange("p a t -> p (a t)"),
                                         ACT.Square).then_inc(sq_ready, 1)
            split_hi(JG + 1, JG // 2, 1)
            def chunk(c, last):
                jh = c * KT + JG // 2
                with act.Fori(0, KT // 2) as i:
                    for s in range(2):
                        j, m = c * 2 * KT + i * 2 + JG + s, c * KT + i * 2 + s
                        act.wait_ge(set_free[s], jh + i + 2)
                        nc.scalar.activation(tmp[:, s, :], tmp[:, s, :], ACT.Square).then_inc(r_ready, 1)
                        act.wait_ge(r_ready, m + 1)
                        copy(r_hi[:, ds(i * 2 + s, 1), :].rearrange("p a t -> p (a t)"), tmp[:, s, :]).then_inc(r_hi_ready, 1)
                        split_hi(j + 2, jh + i + 1, s)
                with act.Fori(0, KT // 2 - last) as i:
                    for s in range(2):
                        split_hi(c * 2 * KT + i * 2 + JG + KT + s + 2, jh + i + KT // 2 + 1, s)

            with act.Fori(0, NC - 1) as c:
                chunk(c, False)
            act.dma_start(gf_row[:, :], lnf_g.rearrange("(a n) -> a n", a=1).to_broadcast([P, D])).then_inc(gf_in, 16)
            chunk(NC - 1, True)
            for t in range(NTOK):
                r, bank = ROWS[t], 2 * (t % 3)
                act.wait_ge(y_turned, t + 1)
                if t >= 1:
                    act.wait_ge(y_sq, t)
                square(tmp[0:r, 0, 0:D].rearrange("p (a b) -> p a b", a=2), ps[0:r, bank:bank + 2, :], t).then_inc(y_sq, 1)

        @block.vector
        def _(dve):
            chain = Chain(dve, chain_v)
            tt, ts, cp = nc.vector.tensor_tensor, nc.vector.tensor_scalar, nc.vector.tensor_copy

            def gain(t):
                r, bank = ROWS[t], 2 * (t % 3)
                dve.wait_ge(xt_done, t + 1)
                if t >= 2:
                    dve.wait_ge(xn_done, t - 1)
                tt(xg[:, t % 2, :, 0:r], ps[:, bank:bank + 2, :].rearrange("p a (k q) -> p (a k) q", q=P)[:, :, 0:r],
                   g1[:, :].unsqueeze(2).to_broadcast([P, KT, r]), ALU.mult).then_inc(xg_done, 1)

            dve.wait_ge(small_in, 64)
            ts(nsink[:, :], nsink[:, :], -1.0, None, ALU.mult).then_inc(nsink_ready, 1)
            for t in range(NTOK):
                r = ROWS[t]
                dve.wait_ge(rstd_done, t + 1)
                ts(x_stage[0:r, t, :], x_stage[0:r, t, :], rstd[0:r, t:t + 1], None, ALU.mult).then_inc(xs_done, 1)
                if t >= 1:
                    gain(t - 1)
            gain(NTOK - 1)

            def split_lo(j, s):
                dve.wait_ge(w_hi_ready, j + 1)
                tt(w_lo[:, s], raw[:, s], w_hi[:, s].bitcast(F32), ALU.subtract).then_inc(w_split, 1)

            split_lo(0, 0)

            def mask(u, slot, b):
                lo = P if b == 0 else 0
                dve.wait_ge(scores_ready, u + 1)
                dve.wait_ge(probs_turned, u + 1)
                cp(prob[:, slot, :, 2 * P], nsink_g[:, :])
                for h in range(HPG):
                    c = (h % 2) * 2 * P
                    last = nc.vector.tensor_tensor_reduce(
                        out=prob[:, slot, h, lo:2 * P], in0=ps[:, 2 * slot + h // 2, c + lo:c + 2 * P],
                        in1=abias[:, h, lo:2 * P], scale=-SCALE, scalar=nsink_g[:, h:h + 1],
                        op0=ALU.add, op1=ALU.min, accum_out=nmax[:, slot, h:h + 1])
                last.then_inc(scores_masked, 1)

            def recip(u, slot):
                dve.wait_ge(exp_done, u + 1)
                nc.vector.reciprocal(rden[:, slot, :], den[:, slot, :]).then_inc(rden_done, 1)

            def move_pt(u, slot, b):
                dve.wait_ge(probs_turned, u + 3)
                dve.wait_ge(pv_done, u + 1)
                if b == 0:
                    dve.sem_inc(pt_v, 1)
                else:
                    cp(p_t[:, slot, 0, :, :], ps[:, 4, :].rearrange("p (h q) -> p h q", h=HPG)).then_inc(pt_v, 1)

            def out_lo(u, g, b):
                dve.wait_ge(o_hi, u + 1)
                for par in range(2):
                    rows = slice(par * HD, (par + 1) * HD)
                    src = ps[rows, 6, :].rearrange("p (t r q) -> p r t q", t=2, r=2)[:, par]
                    at_ = (rows, ds(g * 2, 2), slice(b * P, (b + 1) * P))
                    last = tt(b_lo[at_], src, b_hi[at_].bitcast(F32), ALU.subtract)
                last.then_inc(o_lo, 1)

            def q_low(g, s, pair):
                dve.wait_ge(q_hi_ready, g * 2 + pair + 1)
                for par in range(2):
                    h = 2 * pair + par
                    rows = slice(par * HD, (par + 1) * HD)
                    tt(by3(q_st[HD:P, h, :]), pset(s, rows), by3(q_st[0:HD, h, :]).bitcast(F32), ALU.subtract)
                    last = cp(q_dec[:, :, ds(g * HPG + h, 1)], ps[rows, 3 * s + 2, TN - NB:TN].unsqueeze(2))
                last.then_inc(set_free[s], 1)

            with dve.Fori(0, NG // 2) as gp:
                for g2_ in range(2):
                    g, u0 = gp * 2 + g2_, gp * 2 * NBLK + g2_ * NBLK
                    L = 3 * g2_
                    s = L % 2
                    split_lo(gp * 6 + L + 1, 1 - s)
                    dve.wait_ge(k_hi_ready, g + 1)
                    for half in range(2):
                        rows = slice(half * HD, (half + 1) * HD)
                        tt(by3(k_lo[rows, :]), pset(s, slice(0, HD)), by3(k_hi[rows, :]).bitcast(F32), ALU.subtract)
                    cp(k_dec[:, ds(g, 1), :], ps[0:HD, 3 * s + 2, TN - NB:TN].unsqueeze(1))
                    cp(v_dec[:, ds(g, 1), :], ps[HD:P, 3 * s + 2, TN - NB:TN].unsqueeze(1)).then_inc(set_free[s], 1)
                    split_lo(gp * 6 + L + 2, s)
                    q_low(g, 1 - s, 0)
                    dve.wait_ge(kv_turned, g * 2 + 1)
                    for half in range(2):
                        for bank in range(2):
                            last = cp(v_dup[:, 4 * bank:4 * bank + 4, half * HD:(half + 1) * HD],
                                      ps[:, 6 + bank, :].rearrange("p (t c) -> p t c", t=4)[:, :, HD:P])
                    last.then_inc(v_moved, 1)
                    dve.wait_ge(tail_out, g * 64 + 64)
                    cp(kv_tail[:, 0, :], ps[:, 7, 3 * P:4 * P]).then_inc(tail_ready, 1)
                    split_lo(gp * 6 + L + 3, 1 - s)
                    q_low(g, s, 1)
                    dve.wait_ge(kv_turned, g * 2 + 2)
                    cp(kv_tail[0:NB, 1, :], ps[0:NB, 6, 0:P]).then_inc(tail_ready, 1)
                    dve.wait_ge(abias_ready, g + 1)
                    mask(u0, 0, 0)
                    mask(u0 + 1, 1, 1)
                    recip(u0, 0)
                    for b in range(NBLK):
                        move_pt(u0 + b, b % 2, b)
                        if b + 1 < NBLK:
                            recip(u0 + b + 1, (b + 1) % 2)
                        if b + 2 < NBLK:
                            mask(u0 + b + 2, b % 2, b + 2)
                        if b >= 1:
                            out_lo(u0 + b - 1, g, b - 1)
                    out_lo(u0 + NBLK - 1, g, NBLK - 1)

            dve.wait_ge(pv_done, NU + 2)
            for col, row in ((slopes, slope_row), (nsink, nsink_row)):
                chain.link(tt(dself[:, :].rearrange("p (b h) -> p b h", b=NB), ident[:, :].rearrange("p (b h) -> p b h", b=NB),
                              col[:, :].unsqueeze(1).to_broadcast([P, NB, H]), ALU.mult))
                chain.link(nc.vector.reduce_sum(row[:, :], dself[:, :], axis=mybir.AxisListType.X))
            dve.wait_ge(dbias_ready, 1)
            ts(dbias[:, :], dbias[:, :], slope_row[:, 0:1], None, ALU.mult)
            cp(dprob[:, W + 1:W + 2], nsink_row[:, :])
            tt(prod_t[:, :, :].rearrange("p b (g h) -> p b g h", g=NG), q_dec[:, :, :].rearrange("p b (g h) -> p b g h", g=NG),
               k_dec[:, :, :].rearrange("p g b -> p b g").unsqueeze(3).to_broadcast([HD, NB, NG, HPG]),
               ALU.mult).then_inc(dprod_ready, 1)
            dve.wait_ge(dst_done, NB)
            cp(st_sb[:, :], ps[:, 5, 0:P]).then_inc(dst_moved, 1)
            dve.wait_ge(ds_ready, 1)
            nc.vector.tensor_tensor_reduce(out=dprob[:, 0:W + 1], in0=ps[:, 4, 0:W + 1], in1=dbias[:, :],
                                           scale=-SCALE, scalar=nsink_row[:, 0:1], op0=ALU.add, op1=ALU.min,
                                           accum_out=dstat[:, 0:1]).then_inc(dmasked, 1)
            dve.wait_ge(dexp, 1)
            chain.link(nc.vector.reciprocal(dstat[:, 2:3], dstat[:, 1:2]))
            chain.link(ts(dprob[:, 0:W + 1], dprob[:, 0:W + 1], dstat[:, 2:3], None, ALU.mult))
            ts(dself[:, :], ident[:, :], dprob[:, W:W + 1], None, ALU.mult).then_inc(dprobs, 1)
            dve.wait_ge(dp_turned, 1)
            cp(dp_t[:, :, :].rearrange("p b h -> p (b h)"), ps[:, 3, 0:P]).then_inc(dp_moved, 1)
            dve.wait_ge(dpv_done, 1)
            vb = v_dec[:, :, :].rearrange("p g b -> p b g").unsqueeze(3).to_broadcast([HD, NB, NG, HPG])
            chain.link(tt(d_o[0:HD].rearrange("p b (g h) -> p b g h", g=NG),
                          ps[0:HD, 7, 0:P].rearrange("p (b g h) -> p b g h", b=NB, g=NG), vb, ALU.mult))
            flat = d_o[0:HD].rearrange("p b h -> p (b h)")
            chain.link(tt(flat, ps[0:HD, 6, 0:P], flat, ALU.add))
            cp(d_o[HD:P], d_o[0:HD]).then_inc(do_ready, 1)
            dve.wait_ge(db_hi, 1)
            for par in range(2):
                rows = slice(par * HD, (par + 1) * HD)
                last = tt(b_lo[rows, :, SEQ:T], d_o[rows].rearrange("p b (t r) -> p r t b", r=2)[:, par],
                          b_hi[rows, :, SEQ:T].bitcast(F32), ALU.subtract)
            last.then_inc(db_ready, 1)

            with dve.Fori(0, KT) as n:
                j = n * 2 + JB
                split_lo(j + 1, 1)
                split_lo(j + 2, 0)
                dve.wait_ge(set_free[0], n + JB // 2 + 2)
                dve.wait_ge(job_done, j + 3)
                tt(by3(h_f[:, ds(n, 1), :].rearrange("p a t -> p (a t)")), by3(tmp[:, 0, :]), pset(1),
                   ALU.mult).then_inc(set_free[1], 1)

            def variances(bank):
                ts(var[:, 0:NBLK], ps[:, bank, 0:NBLK], 1.0 / D, EPS, ALU.mult, ALU.add)
                return ts(var[0:NB, NBLK:], ps[0:NB, bank, NBLK:NTOK], 1.0 / D, EPS, ALU.mult, ALU.add)

            dve.wait_ge(set_free[1], JC // 2 + 1)
            with dve.Fori(0, KT // 2) as i:
                for s in range(2):
                    split_lo(i * 2 + JC + s + 1, 1 - s)
                    dve.wait_ge(set_free[s], i + JC // 2 + 2)
                    dve.wait_ge(v_sq_added, i * 2 + s + 1)
                    v_ = mix[:, ds(i * 2 + s, 1), :].rearrange("p a t -> p (a t)")
                    tt(tmp[:, s, :], v_, v_, ALU.mult).then_inc(v_sq, 1)
            dve.wait_ge(sgu_in, 64)
            tt(wt_dec[:, :, :], ident[0:NB, 0:NB].unsqueeze(1).to_broadcast([NB, GS, NB]),
               wt00[:, :].unsqueeze(2).to_broadcast([NB, GS, NB]), ALU.mult)
            dve.wait_ge(wt_turned, 1)
            cp(wt[:, :, :], ps[:, 6:8, :].rearrange("p a (g q) -> p (a g) q", q=P)).then_inc(wt_ready, 1)

            def scale_mix(t):
                r, bank = ROWS[t], 4 + 2 * (t % 2)
                dve.wait_ge(mixed, t + 1)
                tt(mix[:, :, toks(t)], ps[:, bank:bank + 2, :].rearrange("p a (k q) -> p (a k) q", q=P)[:, :, 0:r],
                   gv[:, :].unsqueeze(2).to_broadcast([P, KT, r]), ALU.mult).then_inc(scaled, 1)

            dve.wait_ge(v_ss, 1)
            variances(6).then_inc(v_var, 1)
            for t in range(NTOK):
                scale_mix(t)
            dve.wait_ge(vn_ready, NTOK)
            tt(vs_out[:, :], vn[0:NB, NBLK % 2, :], gv_row[:, :], ALU.mult).then_inc(vs_ready, 1)

            dve.wait_ge(mix_ready, NTOK)
            dve.wait_ge(vs_stored, 16)
            with dve.Fori(0, KT // 2) as i:
                for s in range(2):
                    n = i * 2 + s
                    split_lo(i * 2 + JD + s + 1, 1 - s)
                    dve.wait_ge(set_free[s], i + JD // 2 + 2)
                    tt(tmp[:, s, :], tmp[:, s, :], mix[:, ds(n, 1), :].rearrange("p a t -> p (a t)"), ALU.mult).then_inc(a_ready, 1)
                    dve.wait_ge(a_hi_ready, n + 1)
                    tt(a_lo[:, ds(n, 1), :].rearrange("p a t -> p (a t)"), tmp[:, s, :],
                       a_hi[:, ds(n, 1), :].rearrange("p a t -> p (a t)").bitcast(F32), ALU.subtract).then_inc(a_lo_ready, 1)

            with dve.Fori(0, KT) as n:
                j = n * 2 + JE
                split_lo(j + 1, 1)
                split_lo(j + 2, 0)
                dve.wait_ge(set_free[0], n + JE // 2 + 2)
                dve.wait_ge(h_ready, n + 1)
                dve.wait_ge(job_done, j + 3)
                tt(by3(tmp[:, 1, :]), by3(tmp[:, 0, :]), pset(1), ALU.mult).then_inc(set_free[1], 1)

            for n in range(KT):
                dve.wait_ge(h_hi_ready, n + 1)
                tt(h_lo[:, n, :], h_f[:, n, :], h_hi[:, n, :].bitcast(F32), ALU.subtract).then_inc(h_split, 1)
            for t in range(1, NTOK, 2):
                bank = 2 * (t % 3)
                dve.wait_ge(xr_turned, t + 1)
                cp(res[:, :, toks(t)], ps[:, bank:bank + 2, :].rearrange("p a (k q) -> p (a k) q", q=P)).then_inc(xr_moved[1], 1)
            dve.wait_ge(xr_moved[0], (NTOK + 1) // 2)
            dve.wait_ge(xr_moved[1], NTOK // 2)

            def add_res(n, s):
                r_ = by3(res[:, ds(n, 1), :].rearrange("p a t -> p (a t)"))
                tt(r_, pset(s), r_, ALU.add).then_inc(set_free[s], 1)

            with dve.Fori(0, KT // 2) as i:
                for s in range(2):
                    j = i * 2 + JF + s
                    split_lo(j + 1, 1 - s)
                    dve.wait_ge(job_done, j + 2)
                    add_res(i * 2 + s, s)
                    dve.wait_ge(xf_hi_ready, i * 2 + s + 1)
                    nc.vector.scalar_tensor_tensor(
                        out=xf_lo[:, ds(i * 2 + s, 1), :].rearrange("p a t -> p (a t)"),
                        in0=res[:, ds(i * 2 + s, 1), :].rearrange("p a t -> p (a t)"), scalar=g2[:, ds(i * 2 + s, 1)],
                        in1=xf_hi[:, ds(i * 2 + s, 1), :].rearrange("p a t -> p (a t)").bitcast(F32),
                        op0=ALU.mult, op1=ALU.subtract).then_inc(xf_split, 1)
            split_lo(JG + 1, 1)
            dve.wait_ge(ss_ready, 1)
            variances(6).then_inc(var_ready, 1)
            for n, (bank, t0, t1) in enumerate(RB):
                dve.wait_ge(rb_ready, n + 1)
                w_ = min(t1 * P, T) - t0 * P
                cp(rstd_b[:, t0 * P:t0 * P + w_], ps[:, bank, 0:w_]).then_inc(rb_moved, 1)
            dve.wait_ge(rb_moved, len(RB))

            def chunk(c, last):
                with dve.Fori(0, KT // 2) as i:
                    for s in range(2):
                        j, m = c * 2 * KT + i * 2 + JG + s, c * KT + i * 2 + s
                        dve.wait_ge(job_done, j + 2)
                        dve.wait_ge(r_split, m + 1)
                        nc.vector.scalar_tensor_tensor(
                            out=by3(tmp[:, s, :]), in0=pset(s), scalar=0.0, in1=by3(rstd_b[:, :]),
                            op0=ALU.max, op1=ALU.mult).then_inc(set_free[s], 1)
                        dve.wait_ge(r_hi_ready, m + 1)
                        tt(r_lo[:, ds(i * 2 + s, 1), :].rearrange("p a t -> p (a t)"), tmp[:, s, :],
                           r_hi[:, ds(i * 2 + s, 1), :].rearrange("p a t -> p (a t)").bitcast(F32),
                           ALU.subtract).then_inc(r_split, 1)
                        split_lo(j + 2, s)
                with dve.Fori(0, KT // 2 - last) as i:
                    for s in range(2):
                        j = c * 2 * KT + i * 2 + JG + KT + s
                        dve.wait_ge(job_done, j + 2)
                        add_res(i * 2 + s, s)
                        split_lo(j + 2, s)
                if last:
                    for s in range(2):
                        dve.wait_ge(job_done, JN + s)
                        add_res(KT - 2 + s, s)

            with dve.Fori(0, NC - 1) as c:
                chunk(c, False)
            chunk(NC - 1, True)
            dve.wait_ge(gf_in, 16)
            for t in range(NTOK):
                r, bank = ROWS[t], 2 * (t % 3)
                dve.wait_ge(y_rstd, t + 1)
                if t >= 2:
                    dve.wait_ge(y_stored[t % 2], 16 * (t // 2))
                nc.vector.scalar_tensor_tensor(
                    out=y_t[0:r, t % 2, :].rearrange("p (a b) -> p a b", a=2), in0=ps[0:r, bank:bank + 2, :],
                    scalar=rstd[0:r, t:t + 1], in1=gf_row[0:r, :].rearrange("p (a b) -> p a b", a=2),
                    op0=ALU.mult, op1=ALU.mult).then_inc(y_ready, 1)

        @block.tensor
        def _(pe):
            mm = nc.tensor.matmul

            def turn(out, in_, r=P):
                return nc.tensor.transpose(out, in_, ident[0:r, 0:r])

            def job(j, h, s, hi, lo, ready=None, banks_first=False):
                pe.wait_ge(w_split, j + 3)
                pe.wait_ge(set_free[s], h + 1)
                passes = ((w_hi, hi), (w_hi, lo), (w_lo, hi))
                order = [(k, n, b) for k in range(KT) for n in range(3) for b in range(NT)]
                if banks_first:
                    order = [(k, n, b) for b in range(NT) for k in range(KT) for n in range(3)]
                seen = None
                for k, n, b in order:
                    at_ = b if banks_first else k
                    if ready and at_ != seen:
                        ready(at_)
                        seen = at_
                    w, x = passes[n]
                    last = mm(ps[:, 3 * s + b, 0:TN], w[:, s, k, :], x[:, k, b * TN:(b + 1) * TN],
                              start=(k == 0 and n == 0), stop=(k == KT - 1 and n == 2))
                last.then_inc(job_done, 1)

            pe.wait_ge(const_ready, 1)
            for t in range(NTOK):
                r, bank = ROWS[t], 2 * (t % 3)
                pe.wait_ge(xs_done, t + 1)
                if t >= 3:
                    pe.wait_ge(xg_done, t - 2)
                for k in range(KT):
                    last = turn(ps[:, bank + k // 4, (k % 4) * P:(k % 4) * P + r], x_stage[0:r, t, k * P:(k + 1) * P], r)
                last.then_inc(xt_done, 1)

            def scores(u, slot, b):
                lo = P if b == 0 else 0
                pe.wait_ge(scores_masked, u + 1)
                keys = slice((b - 1) * P + lo, (b + 1) * P)
                for h in range(HPG):
                    c = (h % 2) * 2 * P
                    for n, k_ in enumerate((k_hi, k_lo)):
                        last = mm(ps[:, 2 * slot + h // 2, c + lo:c + 2 * P], q_st[:, h, b * P:(b + 1) * P],
                                  k_[:, keys], start=(n == 0), stop=(n == 1))
                last.then_inc(scores_ready, 1)

            def turn_probs(u, slot, b):
                pe.wait_ge(probs_ready, u + 1)
                pe.wait_ge(pt_a, u + 1)
                pe.wait_ge(pt_v, u + 1)
                for kb in range(1 if b == 0 else 0, 2):
                    for h in range(HPG):
                        last = turn(ps[:, 4 + kb, h * P:(h + 1) * P], prob[:, slot, h, kb * P:(kb + 1) * P])
                last.then_inc(probs_turned, 1)

            def values(u, slot, b):
                pe.wait_ge(pt_a, u + 2)
                pe.wait_ge(pt_v, u + 2)
                pe.wait_ge(o_lo, u + 1)
                first = 1 if b == 0 else 0
                for kb in range(first, 2):
                    last = mm(ps[:, 6, :], v_dup[:, b - 1 + kb, :], p_t[:, slot, kb, :, :].rearrange("p h q -> p (h q)"),
                              start=(kb == first), stop=(kb == 1))
                last.then_inc(pv_done, 1)

            def kv_head(gp, g2_, first=False):
                g, u0 = gp * 2 + g2_, gp * 2 * NBLK + g2_ * NBLK
                L = 3 * g2_

                def the_job(n):
                    job(gp * 6 + n, gp * 3 + n // 2, n % 2, xn_hi, xn_lo,
                        (lambda b: pe.wait_ge(xn_done, min(NTOK, -(-(b + 1) * TN // P)))), True)

                the_job(L)
                the_job(L + 1)
                pe.wait_ge(kv_t_ready, g + 1)
                for t in range(NBLK):
                    last = turn(ps[:, 6 + t // 4, (t % 4) * P:(t % 4 + 1) * P], kv_t[:, t * P:(t + 1) * P])
                last.then_inc(kv_turned, 1)
                the_job(L + 2)
                pe.wait_ge(v_moved, g + 1)
                turn(ps[0:NB, 6, 0:P], kv_t[:, SEQ:T]).then_inc(kv_turned, 1)
                for n in range(L, L + 3):
                    pe.wait_ge(set_free[n % 2], gp * 3 + n // 2 + 2)
                scores(u0, 0, 0)
                scores(u0 + 1, 1, 1)
                pe.wait_ge(tail_ready, g * 2 + 2)
                for b in range(NBLK):
                    if b + 2 < NBLK and b >= 0:
                        pass
                    turn_probs(u0 + b, b % 2, b)
                    if b + 2 < NBLK:
                        scores(u0 + b + 2, b % 2, b + 2)
                    if b >= 1:
                        values(u0 + b - 1, (b - 1) % 2, b - 1)
                values(u0 + NBLK - 1, (NBLK - 1) % 2, NBLK - 1)

            with pe.Fori(0, NG // 2) as gp:
                for g2_ in range(2):
                    kv_head(gp, g2_)

            pe.wait_ge(cache_in, 32)
            pe.wait_ge(o_lo, NU + 1)
            for b in range(NB + 1):
                if b < NB:
                    if b >= 2:
                        pe.wait_ge(dk_moved, b - 1)
                    for g in range(NG):
                        last = turn(ps[0:HD, 6 + b % 2, g * P:(g + 1) * P], ck[:, b, g * HD:(g + 1) * HD])
                    last.then_inc(dk_turned, 1)
                if b >= 1:
                    pe.wait_ge(dk_moved, b)
                    for g in range(NG):
                        c = (b - 1) * H + g * HPG
                        last = mm(ps[:, 5, c:c + HPG], ck_t[:, (b - 1) % 2, g, :], q_dec[:, b - 1, g * HPG:(g + 1) * HPG],
                                  start=True, stop=True)
                    last.then_inc(dst_done, 1)
            pe.wait_ge(dst_moved, 1)
            pe.wait_ge(dprod_ready, 1)
            turn(ps[:, 4, 0:P], st_sb[:, :])
            mm(ps[:, 4, P:P + 1], prod_t[:, :, :].rearrange("p b h -> p (b h)"), ones[0:HD, 0:1],
               start=True, stop=True).then_inc(ds_ready, 1)
            pe.wait_ge(dprobs, 1)
            turn(ps[:, 3, 0:P], dprob[:, 0:W])
            mm(ps[0:HD, 7, 0:P], ones[:, 0:HD], dself[:, :], start=True, stop=True).then_inc(dp_turned, 1)
            pe.wait_ge(dp_moved, 1)
            for b in range(NB):
                for g in range(NG):
                    c = b * H + g * HPG
                    last = mm(ps[0:HD, 6, c:c + HPG], cv[:, b, g * HD:(g + 1) * HD], dp_t[:, b, g * HPG:(g + 1) * HPG],
                              start=True, stop=True)
            last.then_inc(dpv_done, 1)

            with pe.Fori(0, KT) as n:
                job(n * 2 + JB, n + JB // 2, 0, xn_hi, xn_lo)
                pe.wait_ge(db_ready, 1)
                job(n * 2 + JB + 1, n + JB // 2, 1, b_hi, b_lo)
            with pe.Fori(0, KT // 2 - 1) as i:
                for s in range(2):
                    job(i * 2 + JC + s, i + JC // 2, s, xn_hi, xn_lo)
            pe.wait_ge(sgu_masked, 1)
            for g in range(GS):
                last = turn(ps[:, 6 + g // 4, (g % 4) * P:(g % 4 + 1) * P], sgu_raw[:, g, :])
            last.then_inc(wt_turned, 1)
            for s in range(2):
                job(JD - 2 + s, JD // 2 - 1, s, xn_hi, xn_lo)
            for s in range(2):
                pe.wait_ge(set_free[s], JD // 2 + 1)

            def sums(bank):
                for t in range(NTOK):
                    last = mm(ps[0:ROWS[t], bank, t:t + 1], sq_sum[:, toks(t)], ones[:, 0:1], start=True, stop=True)
                return last

            def turn_v(t):
                r, bank = ROWS[t], 2 * (t % 2)
                if t >= 2:
                    pe.wait_ge(vn_ready, t - 1)
                for k in range(KT):
                    last = turn(ps[0:r, bank + k // 4, (k % 4) * P:(k % 4 + 1) * P], mix[:, k, toks(t)])
                last.then_inc(vt_turned, 1)

            turn_v(0)
            pe.wait_ge(v_sq_added, KT + 2)
            pe.wait_ge(wt_ready, 1)
            sums(6).then_inc(v_ss, 1)
            turn_v(1)
            pe.wait_ge(v_var, 1)
            for t in range(NTOK):
                r, bank = ROWS[t], 4 + 2 * (t % 2)
                pe.wait_ge(vn_ready, t + 1)
                if t >= 2:
                    pe.wait_ge(scaled, t - 1)
                for g in range(GS):
                    w_ = wt[:, g, :] if t < NBLK else wt_dec[:, g, :]
                    last = mm(ps[:, bank + g // 4, (g % 4) * P:(g % 4) * P + r], vn[0:r, t % 2, g * P:(g + 1) * P], w_,
                              start=True, stop=True)
                last.then_inc(mixed, 1)
                if t + 2 < NTOK:
                    turn_v(t + 2)
            pe.wait_ge(scaled, NTOK)
            with pe.Fori(0, KT // 2) as i:
                for s in range(2):
                    job(i * 2 + JD + s, i + JD // 2, s, xn_hi, xn_lo)
            with pe.Fori(0, KT) as n:
                job(n * 2 + JE, n + JE // 2, 0, xn_hi, xn_lo)
                pe.wait_ge(a_lo_ready, KT + 2)
                job(n * 2 + JE + 1, n + JE // 2, 1, a_hi, a_lo)
            for s in range(2):
                pe.wait_ge(set_free[s], JF // 2 + 1)
            for t in range(NTOK):
                r, bank = ROWS[t], 2 * (t % 3)
                pe.wait_ge(x_in[t], 32)
                if t >= 3:
                    pe.wait_ge(xr_moved[(t - 3) % 2], (t - 3) // 2 + 1)
                src = x_again[:, t, :] if t < NBLK else x_dec[:, :]
                for k in range(KT):
                    last = turn(ps[:, bank + k // 4, (k % 4) * P:(k % 4) * P + r], src[:, k * P:(k + 1) * P], r)
                last.then_inc(xr_turned, 1)
            pe.wait_ge(xr_moved[0], (NTOK + 1) // 2)
            pe.wait_ge(xr_moved[1], NTOK // 2)
            with pe.Fori(0, KT // 2) as i:
                for s in range(2):
                    job(i * 2 + JF + s, i + JF // 2, s, h_hi, h_lo, lambda k: pe.wait_ge(h_split, k + 1))
            def up(c, i, s, wait=True):
                job(c * 2 * KT + i * 2 + JG + s, c * KT + i + JG // 2, s, xf_hi, xf_lo,
                    (lambda k: pe.wait_ge(xf_split, k + 1)) if wait else None)

            def down(c):
                with pe.Fori(0, KT // 2) as i:
                    for s in range(2):
                        job(c * 2 * KT + i * 2 + JG + KT + s, c * KT + i + (JG + KT) // 2, s, r_hi, r_lo,
                            lambda k: pe.wait_ge(r_split, c * KT + k + 3))

            up(0, 0, 0)
            pe.wait_ge(sq_added, KT + 2)
            sums(6).then_inc(ss_ready, 1)
            up(0, 0, 1, False)
            pe.wait_ge(rs_ready, 1)
            for n, (bank, t0, t1) in enumerate(RB):
                if n >= 2:
                    pe.wait_ge(rb_moved, n - 1)
                for t in range(t0, t1):
                    r = ROWS[t]
                    last = mm(ps[:, bank, (t - t0) * P:(t - t0) * P + r], rstd[0:r, t:t + 1].to_broadcast([r, P]),
                              ident[0:r, 0:r], start=True, stop=True)
                last.then_inc(rb_ready, 1)
            with pe.Fori(1, KT // 2) as i:
                for s in range(2):
                    up(0, i, s, False)
            down(0)
            with pe.Fori(1, NC) as c:
                with pe.Fori(0, KT // 2) as i:
                    for s in range(2):
                        up(c, i, s, False)
                down(c)
            for s in range(2):
                pe.wait_ge(set_free[s], JN // 2 + 1)
            for t in range(NTOK):
                r, bank = ROWS[t], 2 * (t % 3)
                if t >= 3:
                    pe.wait_ge(y_ready, t - 2)
                for k in range(KT):
                    last = turn(ps[0:r, bank + k // 4, (k % 4) * P:(k % 4 + 1) * P], res[:, k, toks(t)])
                last.then_inc(y_turned, 1)


_INS = ["x_prompt", "x_sample", "cache_k_win", "cache_v_win", "ln1_g", "w_in", "sgu_norm_g", "sgu_w", "sgu_b",
        "attn_sinks", "w_oa", "w_ob", "w_out", "ln2_g", "w_up", "w_down", "lnf_g"]


def kernel(**inputs):
    import numpy as np
    import concourse.bacc as bacc
    from concourse.bass_utils import run_bass_kernel_spmd

    nc = bacc.Bacc("TRN2", target_bir_lowering=False, num_devices=1)
    arrays, ins = {}, []
    for name in _INS:
        a = np.ascontiguousarray(inputs[name])
        arrays["in_" + name] = a
        ins.append(nc.dram_tensor("in_" + name, a.shape, mybir.dt.from_np(a.dtype), kind="ExternalInput").ap())
    xp, xs, ck = (arrays["in_" + n].shape for n in ("x_prompt", "x_sample", "cache_k_win"))
    window = min(ck[2], xp[1])
    shapes = [("y_prompt", xp), ("y_sample", xs),
              ("k_win_p", (ck[0], xp[0], window) + ck[3:]), ("v_win_p", (ck[0], xp[0], window) + ck[3:]),
              ("k_win_s", ck), ("v_win_s", ck), ("sgu_v_s", (ck[0],) + xs)]
    outs = [nc.dram_tensor("out_" + name, shape, F32, kind="ExternalOutput").ap() for name, shape in shapes]
    build_trunk(nc, *ins, *outs)
    r = run_bass_kernel_spmd(nc, [arrays], core_ids=[0])
    return tuple(r.results[0]["out_" + name] for name, _ in shapes)
```

```python
from contextlib import ExitStack

import concourse.bass as bass
from concourse import mybir
from concourse.alu_op_type import AluOpType as ALU

F32 = mybir.dt.float32
F32R = mybir.dt.float32r
ACT = mybir.ActivationFunctionType
ds = bass.ds


class Chain:

    def __init__(self, eng, sem):
        self.eng, self.sem, self.n, self.local, self.outer = eng, sem, 0, 0, []

    def link(self, instruction):
        instruction.then_inc(self.sem, 1)
        self.local += 1
        self.eng.wait_ge(self.sem, self.n + self.local)

    def enter(self, i, per):
        self.outer.append((self.n + self.local, per))
        self.n, self.local = self.n + self.local + i * per, 0

    def leave(self, turns):
        before, per = self.outer.pop()
        assert self.local == per, self.local
        self.n, self.local = before + turns * per, 0


def build_trunk(nc, x_prompt, x_sample, cache_k, cache_v, ln1_g, w_in, sgu_norm_g, sgu_w, sgu_b,
                sinks, w_oa, w_ob, w_out, ln2_g, w_up, w_down, lnf_g,
                y_prompt, y_sample, k_win_p, v_win_p, k_win_s, v_win_s, sgu_v_s, x_keep):
    P = 128
    SEQ, D = x_prompt.shape[1], x_prompt.shape[2]
    NB = x_sample.shape[0]
    T = SEQ + NB
    NT = 3
    TN = T // NT
    KT = D // P
    NBLK = SEQ // P
    NTOK = NBLK + 1
    W, NG, HD = cache_k.shape[2], cache_k.shape[3], cache_k.shape[4]
    H = sinks.shape[1]
    HPG = H // NG
    GS = sgu_w.shape[1]
    NC = w_up.shape[2] // D
    EPS = 1e-6
    SCALE = float(HD) ** -0.5
    ROWS = [P] * NBLK + [NB]
    assert T == NT * TN and TN <= 512 and W == P and HD == 64 and HPG == 4 and GS == KT and NB * H == P

    OU, OV, OQ = 0, D, 2 * D
    OK = OQ + H * HD
    OVA = OK + NG * HD
    OGA = OVA + NG * HD
    OGB = OGA + D
    w_in, w_oa, w_ob, w_out = w_in[0], w_oa[0], w_ob[0], w_out[0]
    w_up, w_down = w_up[0], w_down[0]

    RB = [(6, NBLK, NTOK), (7, 0, 4), (6, 4, NBLK)]

    JA = 0
    JB = JA + 3 * NG
    JW = JB + KT
    JC = JW + KT
    JD = JC + KT
    JE = JD + KT
    JF = JE + 2 * KT
    JG = JF + KT
    JN = JG + NC * 2 * KT
    NS = (JB + 3) * NT
    NU = NG * NBLK
    assert NBLK == 8 and KT == 8 and NT == 3 and NG % 2 == 0

    with ExitStack() as ctx:
        at = [(nc.sbuf_base + 31) // 32 * 32]

        def region(nbytes):
            start = at[0]
            at[0] += (nbytes + 31) // 32 * 32
            assert at[0] <= nc.sbuf_usable_end, at[0]
            return start

        def place(name, shape, dt, offset):
            return nc.alloc_sbuf_tensor_at(name, shape, dt, offset=offset)

        def sb(name, shape, dt=F32):
            n = 4
            for s in shape[1:]:
                n *= s
            return place(name, shape, dt, region(n))

        ACTB = KT * T * 4
        r_0, r_0b, r_1, r_2, r_3 = (region(ACTB) for _ in range(5))
        xn_hi = place("xn_hi", [P, KT, T], F32R, r_0)
        xn_lo = place("xn_lo", [P, KT, T], F32R, r_0b)
        h_hi = place("h_hi", [P, KT, T], F32R, r_0)
        h_lo = place("h_lo", [P, KT, T], F32R, r_0b)
        r_hi = place("r_hi", [P, KT, T], F32R, r_0)
        r_lo = place("r_lo", [P, KT, T], F32R, r_0b)
        x_stage = place("x_stage", [P, NTOK, D], F32, r_1)
        b_all = place("b_all", [P, KT, T], F32, r_1)
        b_lo = place("b_lo", [P, KT, T], F32R, r_1)
        mix = place("mix", [P, KT, T], F32, r_1)
        a_hi = place("a_hi", [P, KT, T], F32R, r_1)
        res = place("res", [P, KT, T], F32, r_1)
        q_st, k_hi, k_lo, v_dup = [], [], [], []
        for par, r_ in enumerate((r_2, r_3)):
            q_st.append(place(f"q_st{par}", [P, HPG, T], F32R, r_))
            k_hi.append(place(f"k_hi{par}", [P, T], F32R, r_ + 4 * HPG * T))
            k_lo.append(place(f"k_lo{par}", [P, T], F32R, r_ + 4 * (HPG + 1) * T))
            v_dup.append(place(f"v_dup{par}", [P, NBLK, 2 * HD], F32, r_ + 4 * (HPG + 2) * T))
        o = 4 * (HPG + 2) * T + 8 * NBLK * HD
        assert o + 4 * T <= ACTB
        kv_t0 = place("kv_t0", [P, T], F32, r_2 + o)
        p_t = place("p_t", [P, 2, HPG, P], F32, r_3 + o)
        YS = 4
        h_f = place("h_f", [P, KT, T], F32, r_2)
        xf_lo = place("xf_lo", [P, KT, T], F32R, r_2)
        y_t = place("y_t", [P, YS, D], F32, r_2)
        xg = place("xg", [P, 2, KT, P], F32, r_2 + 4 * D)
        x_t = place("x_t", [P, KT, T], F32, r_3)
        CB = NB * NG * HD * 4
        ck = place("ck", [P, NB, NG * HD], F32, r_3)
        cv = place("cv", [P, NB, NG * HD], F32, r_3 + CB)
        ck_t = place("ck_t", [HD, 2, NG, P], F32, r_3 + 2 * CB)
        o = r_3 + 2 * CB + 8 * NG * P
        st_sb = place("st_sb", [P, P], F32, o)
        prod_t = place("prod_t", [HD, NB, H], F32, o + 512)
        dbias = place("dbias", [P, W + 1], F32, o + 1024)
        dprob = place("dprob", [P, W + 2], F32, o + 1024 + 544)
        dp_t = place("dp_t", [P, NB, H], F32, o + 2624)
        dself = place("dself", [P, P], F32, o + 3136)
        d_o = place("d_o", [HD, NB, H], F32, o + 3648)
        assert o + 4160 <= r_3 + ACTB
        b_hi = place("b_hi", [P, KT, T], F32R, r_3)
        a_lo = place("a_lo", [P, KT, T], F32R, r_3)
        xf_hi = place("xf_hi", [P, KT, T], F32R, r_3)
        sgu_raw = place("sgu_raw", [P, GS, P], F32, r_3)
        vn = place("vn", [P, 2, D], F32, r_3 + 4 * D)
        gv_row = place("gv_row", [NB, D], F32, r_3 + 12 * D)
        vs_out = place("vs_out", [NB, D], F32, r_3 + 16 * D)
        wt_dec = place("wt_dec", [NB, GS, NB], F32, r_3 + 20 * D)

        raw = sb("raw", [P, 2, KT, P])
        w_hi = sb("w_hi", [P, 2, KT, P], F32R)
        w_lo = sb("w_lo", [P, 2, KT, P], F32R)

        ident = sb("ident", [P, P])
        ones = sb("ones", [P, P])
        g1, g2, gv = sb("g1", [P, KT]), sb("g2", [P, KT]), sb("gv", [P, KT])
        ssq, var, rstd = sb("ssq", [P, NTOK]), sb("var", [P, NTOK]), sb("rstd", [P, NTOK])
        mhalf = sb("mhalf", [P, NTOK])
        slopes, nsink = sb("slopes", [P, H]), sb("nsink", [P, H])
        nsink_g = sb("nsink_g", [P, HPG])
        slope_row, nsink_row = sb("slope_row", [P, 1]), sb("nsink_row", [P, 1])
        nmax, den, rden = (sb(n, [P, 2, HPG]) for n in ("nmax", "den", "rden"))
        dstat = sb("dstat", [P, 4])
        q_dec = sb("q_dec", [HD, NB, H])
        k_dec, v_dec = sb("k_dec", [HD, NG, NB]), sb("v_dec", [HD, NG, NB])
        wt00 = sb("wt00", [NB, GS])

        o_tmp = 4 * (T + D)
        r_s = region(o_tmp + 3 * T * 4)
        dist8 = place("dist8", [P, 2 * P], F32, r_s)
        abias = place("abias", [P, HPG, 2 * P], F32, r_s + 1024)
        SW = 2 * P + 1
        prob = place("prob", [P, 2, HPG, SW], F32, r_s + 1024 + 8 * HPG * P)
        o = r_s + 1024 + 8 * HPG * P + 8 * HPG * SW
        kv_t = [kv_t0, place("kv_t1", [P, T], F32, o)]
        kv_tail = place("kv_tail", [P, 2, 2 * HD], F32, o + 4 * T)
        assert o + 4 * T + 16 * HD <= at[0]
        wt = place("wt", [P, GS, P], F32, r_s)
        bb = place("bb", [P, GS, P], F32, r_s + 4 * D)
        rstd_b = place("rstd_b", [P, T], F32, r_s)
        gf_row = place("gf_row", [P, D], F32, r_s + 4 * T)
        tmp = place("tmp", [P, 2, T], F32, r_s + o_tmp)
        sq_sum = place("sq_sum", [P, T], F32, r_s + o_tmp + 8 * T)

        ps = ctx.enter_context(nc.psum_tensor("ps", [P, 8, 512], F32))

        def pset(s, rows=slice(0, P)):
            return ps[rows, 3 * s:3 * s + 3, 0:TN]

        def by3(ap):
            return ap.rearrange("p (b t) -> p b t", b=NT)

        def toks(t):
            return slice(t * P, t * P + ROWS[t])

        def sem(name):
            return ctx.enter_context(nc.semaphore(name))

        w_loaded = [sem("w_loaded0"), sem("w_loaded1")]
        w_hi_ready, w_split = sem("w_hi_ready"), sem("w_split")
        job_done = sem("job_done")
        set_free = [sem("set_free0"), sem("set_free1")]
        bank_done, bank_hi, bank_free, gate_free = sem("bank_done"), sem("bank_hi"), sem("bank_free"), sem("gate_free")
        small_in, g1_in = sem("small_in"), sem("g1_in")
        const_ready = sem("const_ready")
        chain_a, chain_v, chain_p = sem("chain_a"), sem("chain_v"), sem("chain_p")
        x_in = [sem(f"x_in{t}") for t in range(NTOK)]
        sq_done, rstd_done, rstd_spread = sem("sq_done"), sem("rstd_done"), sem("rstd_spread")
        xt_done, xt_moved, x_kept = sem("xt_done"), sem("xt_moved"), sem("x_kept")
        xg_done, xn_ready, xhi_done, xn_done = sem("xg_done"), sem("xn_ready"), sem("xhi_done"), sem("xn_done")
        abias_ready = sem("abias_ready")
        kv_turned, v_moved, tail_ready, tail_out = sem("kv_turned"), sem("v_moved"), sem("tail_ready"), sem("tail_out")
        scores_ready, scores_masked = sem("scores_ready"), sem("scores_masked")
        exp_done, rden_done, probs_ready, probs_turned = sem("exp_done"), sem("rden_done"), sem("probs_ready"), sem("probs_turned")
        pt_a, pt_v = sem("pt_a"), sem("pt_v")
        pv_done = sem("pv_done")
        o_moved = sem("o_moved")
        cache_in, dk_turned, dk_moved, dst_ready = sem("cache_in"), sem("dk_turned"), sem("dk_moved"), sem("dst_ready")
        dst_done = sem("dst_done")
        b_hi_ready, b_split = sem("b_hi_ready"), sem("b_split")
        dst_moved, dprod_ready, ds_ready, dmasked, dexp = sem("dst_moved"), sem("dprod_ready"), sem("ds_ready"), sem("dmasked"), sem("dexp")
        dprobs, dp_turned, dp_moved, dpv_done, do_ready, db_ready = (sem(n) for n in ("dprobs", "dp_turned", "dp_moved", "dpv_done", "do_ready", "db_ready"))
        dbias_ready = sem("dbias_ready")
        h_ready, nsink_ready = sem("h_ready"), sem("nsink_ready")
        sgu_in, sgu_masked, wt_turned, wt_ready = sem("sgu_in"), sem("sgu_masked"), sem("wt_turned"), sem("wt_ready")
        vt_turned, v_sq, v_sq_added, v_ss, v_var, v_rstd, vn_ready, mixed, scaled, mix_ready = (sem(n) for n in ("vt_turned", "v_sq", "v_sq_added", "v_ss", "v_var", "v_rstd", "vn_ready", "mixed", "scaled", "mix_ready"))
        vs_ready, vs_stored = sem("vs_ready"), sem("vs_stored")
        u_ready, a_ready, a_hi_ready, a_lo_ready = sem("u_ready"), sem("a_ready"), sem("a_hi_ready"), sem("a_lo_ready")
        h_hi_ready, h_split = sem("h_hi_ready"), sem("h_split")
        res_in = [sem("res_in0"), sem("res_in1")]
        sq_ready, sq_added = sem("sq_ready"), sem("sq_added")
        ss_ready, var_ready, rs_ready, rb_ready, rb_moved = (sem(n) for n in ("ss_ready", "var_ready", "rs_ready", "rb_ready", "rb_moved"))
        xf_hi_ready, xf_split = sem("xf_hi_ready"), sem("xf_split")
        r_ready, r_hi_ready, r_split = sem("r_ready"), sem("r_hi_ready"), sem("r_split")
        y_turned, y_sq, y_sq_added, y_ss, y_var, y_rstd, y_ready = (sem(n) for n in ("y_turned", "y_sq", "y_sq_added", "y_ss", "y_var", "y_rstd", "y_ready"))
        y_stored = [sem(f"y_stored{n}") for n in range(YS)]
        gf_in = sem("gf_in")
        win_stored = sem("win_stored")
        block = ctx.enter_context(nc.Block())

        @block.sync
        def _(sp):
            for t in range(NBLK):
                sp.dma_start(x_stage[:, t, :], x_prompt[0, t * P:(t + 1) * P, :]).then_inc(x_in[t], 16)
            sp.dma_start(x_stage[0:NB, NBLK, :], x_sample[:, 0, :]).then_inc(x_in[NBLK], 16)
            with nc.allow_non_contiguous_dma(reason="gains to partitions, 4 KB each"):
                for dst, src in ((g2, ln2_g[0]), (gv, sgu_norm_g[0])):
                    sp.dma_start(dst[:, :], src.rearrange("(k p) -> p k", p=P)).then_inc(small_in, 16)
            sp.dma_start(nsink[:, :], sinks.to_broadcast([P, H])).then_inc(small_in, 16)
            for dst, src in ((k_win_s, cache_k), (v_win_s, cache_v)):
                sp.dma_start(dst[0, :, 0:W - 1].rearrange("b t g d -> b (t g d)"),
                             src[0, :, 1:W].rearrange("b t g d -> b (t g d)")).then_inc(win_stored, 16)

            def load(j, s, two):
                sp.wait_ge(w_split, j + 1)
                for dst, src in two:
                    sp.dma_start(dst, src).then_inc(w_loaded[s], 16)

            def load_block(j, s, w, row, col):
                halves = w[ds(row, D), ds(col, P)].rearrange("(two k p) n -> two p k n", two=2, p=P)
                load(j, s, [(raw[:, s, h * KT // 2:(h + 1) * KT // 2, :], halves[h]) for h in (1, 0)])

            with sp.Fori(0, NG // 2) as gp:
                for g2_ in range(2):
                    j, g, s = gp * 6 + 3 * g2_, gp * 2 + g2_, g2_ % 2
                    load(j, s, [(raw[:, s, :, half * HD:(half + 1) * HD],
                                 w_in[:, ds(g * HD + col, HD)].rearrange("(k p) n -> p k n", p=P))
                                for half, col in ((0, OK), (1, OVA))])
                    load_block(j + 1, 1 - s, w_in, 0, g * 2 * P + OQ)
                    load_block(j + 2, s, w_in, 0, g * 2 * P + P + OQ)
            for j0, w, col in ((JB, w_in, OGB), (JW, w_ob, 0)):
                with sp.Fori(0, KT // 2) as i:
                    for s in range(2):
                        load_block(i * 2 + j0 + s, s, w, 0, i * 2 * P + s * P + col)
            for j0, col in ((JC, OV), (JD, OU)):
                with sp.Fori(0, KT // 2) as i:
                    for s in range(2):
                        load_block(i * 2 + j0 + s, s, w_in, 0, i * 2 * P + s * P + col)
            with sp.Fori(JE // 2, JE // 2 + KT) as h:
                load_block(h * 2, 0, w_in, 0, (h - JE // 2) * P + OGA)
                load_block(h * 2 + 1, 1, w_oa, 0, (h - JE // 2) * P)
            with sp.Fori(0, KT // 2) as i:
                for s in range(2):
                    load_block(i * 2 + JF + s, s, w_out, 0, i * 2 * P + s * P)
            with sp.Fori(0, NC) as c:
                with sp.Fori(0, KT // 2) as i:
                    for s in range(2):
                        load_block(c * 2 * KT + i * 2 + JG + s, s, w_up, 0, c * D + i * 2 * P + s * P)
                with sp.Fori(0, KT // 2) as i:
                    for s in range(2):
                        load_block(c * 2 * KT + i * 2 + JG + KT + s, s, w_down, c * D, i * 2 * P + s * P)
            for t in range(NTOK):
                sp.wait_ge(y_ready, t + 1)
                dst = y_prompt[0, t * P:(t + 1) * P, :] if t < NBLK else y_sample[:, 0, :]
                sp.dma_start(dst, y_t[0:ROWS[t], t % YS, :]).then_inc(y_stored[t % YS], 16)
            for s in range(YS):
                sp.wait_ge(y_stored[s], 16 * ((NTOK + YS - 1 - s) // YS))
            sp.wait_ge(vs_stored, 16)
            sp.wait_ge(win_stored, 32)
            sp.wait_ge(tail_out, 64 * NG)

        @block.gpsimd
        def _(pool):
            chain = Chain(pool, chain_p)
            pool.sem_inc(w_split, 2)
            pool.sem_inc(job_done, 1)
            pool.sem_inc(set_free[0], JW // 2 + 1)
            pool.sem_inc(set_free[1], JW // 2 + 1)
            pool.sem_inc(bank_free, NT)
            pool.sem_inc(pt_a, 2)
            pool.sem_inc(pt_v, 2)
            pool.sem_inc(o_moved, 1)
            pool.sem_inc(a_lo_ready, 2)
            pool.sem_inc(r_split, 2)
            pool.sem_inc(sq_added, 2)
            pool.sem_inc(v_sq_added, 2)
            pool.sem_inc(y_sq_added, 2)
            pool.sem_inc(h_ready, 1)
            nc.gpsimd.memset(mhalf[:, :], -0.5)
            chain.link(nc.gpsimd.memset(var[:, :], 1.0))
            chain.link(nc.gpsimd.memset(ident[:, :], 0.0))
            nc.gpsimd.affine_select(out=ident[:, :], in_=ident[:, :], compare_op=ALU.not_equal, fill=1.0,
                                    base=0, pattern=[[-1, P]], channel_multiplier=1).then_inc(const_ready, 1)

            for t in range(NTOK):
                r = ROWS[t]
                pool.wait_ge(sq_done, t + 1)
                chain.link(nc.gpsimd.tensor_scalar(var[0:r, t:t + 1], ssq[0:r, t:t + 1], 1.0 / D, EPS,
                                                   ALU.mult, ALU.add))
                nc.gpsimd.tensor_tensor(rstd[0:r, t:t + 1], var[0:r, t:t + 1], mhalf[0:r, 0:1],
                                        ALU.pow).then_inc(rstd_done, 1)
                if t == 0:
                    pool.wait_ge(g1_in, 16)
                pool.wait_ge(xt_moved, t + 1)
                if t >= 2:
                    pool.wait_ge(xn_done, t - 1)
                nc.gpsimd.tensor_tensor(xg[:, t % 2, :, 0:r], x_t[:, :, toks(t)],
                                        g1[:, :].unsqueeze(2).to_broadcast([P, KT, r]), ALU.mult).then_inc(xg_done, 1)

            for h in range(H):
                nc.gpsimd.memset(slopes[:, h:h + 1], 2.0 ** (-8.0 * (h + 1) / H))
            nc.gpsimd.memset(ones[:, :], 1.0)
            chain.link(nc.gpsimd.iota(dist8[:, :], pattern=[[8, 2 * P]], base=-8 * P, channel_multiplier=-8,
                                      allow_small_or_imprecise_dtypes=True))
            chain.link(nc.gpsimd.affine_select(out=dist8[:, :], in_=dist8[:, :], compare_op=ALU.is_ge,
                                               fill=-1e34, base=P, pattern=[[-1, 2 * P]], channel_multiplier=1))
            chain.link(nc.gpsimd.affine_select(out=dist8[:, :], in_=dist8[:, :], compare_op=ALU.is_ge,
                                               fill=-1e34, base=0, pattern=[[1, 2 * P]], channel_multiplier=-1))
            nc.gpsimd.memset(sq_sum[:, 0:1], 0.0).then_inc(const_ready, 1)

            def unit(u, slot, b):
                lo = P if b == 0 else 0
                pool.wait_ge(rden_done, u + 1)
                p = prob[:, slot, :, lo:2 * P]
                nc.gpsimd.tensor_tensor(p, p, rden[:, slot, :].unsqueeze(2).to_broadcast([P, HPG, 2 * P - lo]),
                                        ALU.mult).then_inc(probs_ready, 1)

            pool.wait_ge(nsink_ready, 1)

            def bias(g):
                nc.gpsimd.tensor_copy(nsink_g[:, :], nsink[:, g * HPG:(g + 1) * HPG])
                nc.gpsimd.tensor_tensor(
                    abias[:, :, :], dist8[:, :].unsqueeze(1).to_broadcast([P, HPG, 2 * P]),
                    slopes[:, g * HPG:(g + 1) * HPG].unsqueeze(2).to_broadcast([P, HPG, 2 * P]),
                    ALU.mult).then_inc(abias_ready, 1)

            bias(0)
            for u in range(NU):
                if u % NBLK == NBLK - 1 and u + 1 < NU:
                    pool.wait_ge(scores_masked, u + 1)
                    bias(u // NBLK + 1)
                unit(u, u % 2, u % NBLK)

            pool.wait_ge(pv_done, NU)
            nc.gpsimd.iota(dbias[:, :], pattern=[[8, W + 1]], base=-8 * W, channel_multiplier=0,
                           allow_small_or_imprecise_dtypes=True).then_inc(dbias_ready, 1)

            def add_squares(ready, added):
                def add(n, s):
                    pool.wait_ge(ready, n + 1)
                    pool.wait_ge(added, n + 2)
                    nc.gpsimd.tensor_tensor(sq_sum[:, :], sq_sum[:, :], tmp[:, s, :], ALU.add).then_inc(added, 1)

                with pool.Fori(0, KT // 2 - 1) as i:
                    for s in range(2):
                        add(i * 2 + s, s)
                add(KT - 2, 0)

            def rstd_of_all(done):
                nc.gpsimd.tensor_tensor(rstd[:, :], var[:, :], mhalf[:, :], ALU.pow).then_inc(done, 1)

            def add_bias(t):
                r = ROWS[t]
                pool.wait_ge(scaled, t + 1)
                m = mix[:, :, toks(t)]
                bias = bb[:, :, :] if t < NBLK else bb[:, :, 0:1].to_broadcast([P, GS, r])
                nc.gpsimd.tensor_tensor(m, m, bias, ALU.add).then_inc(mix_ready, 1)

            pool.wait_ge(sgu_in, 64)
            nc.gpsimd.affine_select(out=sgu_raw[:, :, :], in_=sgu_raw[:, :, :], compare_op=ALU.is_ge, fill=0.0,
                                    base=0, pattern=[[0, GS], [-1, P]], channel_multiplier=1).then_inc(sgu_masked, 1)
            pool.wait_ge(tail_out, 64 * NG)
            chain.link(nc.gpsimd.memset(sq_sum[:, :], 0.0))
            add_squares(v_sq, v_sq_added)
            pool.wait_ge(v_var, 1)
            rstd_of_all(v_rstd)
            for t in range(NTOK):
                add_bias(t)

            with pool.Fori(0, KT) as n:
                pool.wait_ge(set_free[1], n + JE // 2 + 2)
                hn = h_f[:, ds(n, 1), :].rearrange("p a t -> p (a t)")
                nc.gpsimd.tensor_tensor(hn, hn, tmp[:, 1, :], ALU.add).then_inc(h_ready, 1)

            chain.link(nc.gpsimd.memset(sq_sum[:, :], 0.0))
            add_squares(sq_ready, sq_added)
            pool.wait_ge(var_ready, 1)
            rstd_of_all(rs_ready)
            pool.wait_ge(ss_ready, 1)
            chain.link(nc.gpsimd.memset(sq_sum[:, :], 0.0))
            add_squares(y_sq, y_sq_added)
            pool.wait_ge(y_var, 1)
            rstd_of_all(y_rstd)

        @block.scalar
        def _(act):
            def copy(dst, src):
                return nc.scalar.activation(dst, src, ACT.Copy)

            def copy_scaled(dst, src, scale):
                return nc.scalar.activation(dst, src, ACT.Copy, scale=scale)

            with nc.allow_non_contiguous_dma(reason="gains to partitions, 4 KB"):
                act.dma_start(g1[:, :], ln1_g[0].rearrange("(k p) -> p k", p=P)).then_inc(g1_in, 16)
            act.wait_ge(const_ready, 1)
            nc.scalar.activation(dstat[:, 3:4], mhalf[:, 0:1], ACT.Square)

            def w_high(j):
                act.wait_ge(w_loaded[j % 2], j // 2 * 32 + 32)
                if j >= 2:
                    act.wait_ge(job_done, j)
                copy(w_hi[:, j % 2], raw[:, j % 2]).then_inc(w_hi_ready, 1)

            def high(t):
                r = ROWS[t]
                act.wait_ge(xn_ready, t + 1)
                copy(xn_hi[:, :, toks(t)], xg[:, t % 2, :, 0:r]).then_inc(xhi_done, 1)

            for t in range(NTOK):
                r, first = ROWS[t], 2 * (t % 3)
                act.wait_ge(x_in[t], 16)
                if t >= 1:
                    act.wait_ge(sq_done, t)
                nc.scalar.activation(tmp[0:r, 0, 0:D], x_stage[0:r, t, :], ACT.Square,
                                     accum_out=ssq[0:r, t:t + 1]).then_inc(sq_done, 1)
                act.wait_ge(xt_done, t + 1)
                copy(x_t[:, :, toks(t)], ps[:, first:first + 2, :].rearrange("p a (k q) -> p (a k) q", q=P)[:, :, 0:r]).then_inc(xt_moved, 1)
                if t >= 1:
                    high(t - 1)
                if t == NBLK - 3:
                    w_high(0)
            high(NTOK - 1)
            act.dma_start(x_keep.rearrange("(k p) t -> p k t", p=P), x_t[:, :, :]).then_inc(x_kept, 16)

            def split_hi(j, h, s):
                act.wait_ge(w_loaded[s], h * 32 + 32)
                act.wait_ge(job_done, j + 0)
                copy(w_hi[:, s], raw[:, s]).then_inc(w_hi_ready, 1)

            def bank_high(n):
                j, b = n // NT, n % NT
                cols = slice(b * TN, (b + 1) * TN)
                act.wait_ge(*((bank_done, 2 * j + b + 1) if b < 2 else (job_done, j + 2)))
                if j >= JB:
                    nc.scalar.activation(h_f[:, j - JB, cols], ps[:, b, 0:TN], ACT.Exp,
                                         scale=-1.0).then_inc(bank_hi if n < NS else gate_free, 1)
                    return
                par, pair = j // 3 % 2, j % 3 - 1
                if pair < 0:
                    copy(kv_t[par][:, cols], ps[:, b, 0:TN])
                    for half in range(2):
                        last = copy(k_hi[par][half * HD:(half + 1) * HD, cols], ps[0:HD, b, 0:TN])
                else:
                    for half in range(2):
                        last = copy(q_st[par][0:HD, 2 * pair + half, cols], ps[half * HD:(half + 1) * HD, b, 0:TN])
                last.then_inc(bank_hi, 1)

            def exps(u):
                slot, lo = u % 2, P if u % NBLK == 0 else 0
                act.wait_ge(scores_masked, u + 1)
                for h in range(HPG):
                    s_ = prob[:, slot, h, lo:SW]
                    last = nc.scalar.activation(s_, s_, ACT.Exp, scale=-1.0, bias=nmax[:, slot, h:h + 1],
                                                accum_out=den[:, slot, h:h + 1])
                last.then_inc(exp_done, 1)

            def move_pt(u):
                act.wait_ge(probs_turned, u + 1)
                if u >= 1:
                    act.wait_ge(pv_done, u)
                copy(p_t[:, 1, :, :], ps[:, 4 + 2 * (u % 2), :].rearrange("p (h q) -> p h q", h=HPG)).then_inc(pt_a, 1)

            def out(u):
                g, b = u // NBLK, u % NBLK
                act.wait_ge(pv_done, u + 1)
                for par in range(2):
                    rows = slice(par * HD, (par + 1) * HD)
                    src = ps[rows, 7, :].rearrange("p (t r q) -> p r t q", t=2, r=2)[:, par]
                    last = copy(b_all[rows, 2 * g:2 * g + 2, b * P:(b + 1) * P], src)
                last.then_inc(o_moved, 1)

            w_high(1)
            for n in range(3 * NT):
                bank_high(n)
                if n in (2, 5):
                    w_high(n // NT + 2)
            act.wait_ge(x_kept, 16)
            for u in range(NU):
                g, b = u // NBLK, u % NBLK
                n, j = (g + 1) * 3 * NT, (g + 1) * 3
                if b == 0:
                    exps(u)
                    bank_high(n)
                move_pt(u)
                if b < NBLK - 1:
                    exps(u + 1)
                bank_high(n + b + 1)
                if b in (0, 2, 5):
                    w_high(j + {0: 1, 2: 2, 5: 3}[b])
                out(u)
                if b == 3:
                    act.wait_ge(tail_ready, g * 2 + 2)
                    for kv, (wp, ws) in enumerate(((k_win_p, k_win_s), (v_win_p, v_win_s))):
                        act.dma_start(ws[0, :, W - 1].rearrange("b g d -> b (g d)")[:, g * HD:(g + 1) * HD],
                                      kv_tail[0:NB, 1, kv * HD:(kv + 1) * HD]).then_inc(tail_out, 16)
                        act.dma_start(wp[0, 0].rearrange("t g d -> t (g d)")[:, g * HD:(g + 1) * HD],
                                      kv_tail[:, 0, kv * HD:(kv + 1) * HD]).then_inc(tail_out, 16)

            act.wait_ge(pv_done, NU)
            for dst, src in ((ck, cache_k), (cv, cache_v)):
                act.dma_start(dst[:, :, :], src[0].rearrange("b w g d -> w b (g d)")).then_inc(cache_in, 16)
            w_high(JB + 4)
            bank_high(NS)
            bank_high(NS + 1)
            for b in range(NB):
                act.wait_ge(dk_turned, b + 1)
                if b >= 2:
                    act.wait_ge(dst_done, b - 1)
                copy(ck_t[:, b % 2, :, :], ps[0:HD, 6 + b % 2, :].rearrange("p (g w) -> p g w", g=NG)).then_inc(dk_moved, 1)
                if b % 2 == 1:
                    bank_high(NS + 2 + b // 2)
                if b == 1:
                    w_high(JB + 5)
            w_high(JB + 6)
            bank_high(NS + 6)
            act.wait_ge(dmasked, 1)
            nc.scalar.activation(dprob[:, :], dprob[:, :], ACT.Exp, scale=-1.0, bias=dstat[:, 0:1],
                                 accum_out=dstat[:, 1:2]).then_inc(dexp, 1)
            bank_high(NS + 7)
            bank_high(NS + 8)
            w_high(JB + 7)
            for n in range(9, 12):
                bank_high(NS + n)
            w_high(JW)
            act.wait_ge(db_ready, 1)
            for k in range(KT):
                copy(b_hi[:, k, :], b_all[:, k, :]).then_inc(b_hi_ready, 1)
                if k in (3, 5, 7):
                    bank_high(NS + 12 + (k - 3) // 2)
            with act.Fori(0, KT // 2) as i:
                for s in range(2):
                    split_hi(i * 2 + JW + s + 1, i + (JW + s + 1) // 2, 1 - s)

            def gates(j0):
                with act.Fori(0, KT) as n:
                    j = n * 2 + j0
                    split_hi(j + 1, n + j0 // 2, 1)
                    act.wait_ge(job_done, j + 2)
                    act.wait_ge(set_free[1], n + j0 // 2 + 1)
                    nc.scalar.activation(by3(tmp[:, 0, :]), pset(0), ACT.Sigmoid).then_inc(set_free[0], 1)
                    split_hi(j + 2, n + j0 // 2 + 1, 0)

            act.wait_ge(job_done, JC + 1)
            act.dma_start(sgu_raw[:, :, :], sgu_w[0].rearrange("g t s -> t g s")).then_inc(sgu_in, 16)
            act.dma_start(bb[:, :, :].rearrange("p g t -> p (g t)"),
                          sgu_b.rearrange("a g t -> a (g t)").to_broadcast([P, GS * P])).then_inc(sgu_in, 16)
            act.dma_start(gv_row[:, :], sgu_norm_g.to_broadcast([NB, D])).then_inc(sgu_in, 16)
            with nc.allow_non_contiguous_dma(reason="one number of each group"):
                act.dma_start(wt00[:, :], sgu_w[0, :, 0, 0:1].rearrange("g s -> s g").to_broadcast([NB, GS])).then_inc(sgu_in, 16)
            with act.Fori(0, KT // 2) as i:
                for s in range(2):
                    j = i * 2 + JC + s
                    split_hi(j + 1, i + (JC + s + 1) // 2, 1 - s)
                    act.wait_ge(job_done, j + 2)
                    nc.scalar.activation(by3(mix[:, ds(i * 2 + s, 1), :].rearrange("p a t -> p (a t)")), pset(s),
                                         ACT.Gelu_apprx_tanh).then_inc(set_free[s], 1)
            act.wait_ge(v_rstd, 1)
            for t in range(NTOK):
                r, bank = ROWS[t], 2 * (t % 2)
                act.wait_ge(vt_turned, t + 1)
                if t >= 2:
                    act.wait_ge(mixed, t - 1)
                nc.scalar.activation(vn[0:r, t % 2, :].rearrange("p (a b) -> p a b", a=2), ps[0:r, bank:bank + 2, :],
                                     ACT.Copy, scale=rstd[0:r, t:t + 1]).then_inc(vn_ready, 1)
            act.wait_ge(vs_ready, 1)
            act.dma_start(sgu_v_s[0, :, 0, :], vs_out[:, :]).then_inc(vs_stored, 16)
            with act.Fori(0, KT // 2) as i:
                for s in range(2):
                    j, n = i * 2 + JD + s, i * 2 + s
                    split_hi(j + 1, i + (JD + s + 1) // 2, 1 - s)
                    act.wait_ge(job_done, j + 2)
                    act.wait_ge(a_lo_ready, n + 1)
                    nc.scalar.activation(by3(tmp[:, s, :]), pset(s), ACT.Gelu_apprx_tanh).then_inc(set_free[s], 1)
                    act.wait_ge(a_ready, n + 1)
                    copy(a_hi[:, ds(n, 1), :].rearrange("p a t -> p (a t)"), tmp[:, s, :]).then_inc(a_hi_ready, 1)
            gates(JE)
            def high_h(n):
                act.wait_ge(h_ready, n + 2)
                copy(h_hi[:, n, :], h_f[:, n, :]).then_inc(h_hi_ready, 1)

            for n in range(KT - 1):
                high_h(n)
            act.wait_ge(job_done, JF + 1)
            for n, (k0, k1) in enumerate(((0, 2), (2, KT))):
                act.dma_start(res[:, k0:k1, :], x_keep[k0 * P:k1 * P, :].rearrange("(k p) t -> p k t", p=P)).then_inc(res_in[n], 16)
            high_h(KT - 1)
            with act.Fori(0, KT // 2) as i:
                for s in range(2):
                    j = i * 2 + JF + s
                    split_hi(j + 1, i + (JF + s + 1) // 2, 1 - s)
                    act.wait_ge(set_free[s], i + JF // 2 + 2)
                    act.wait_ge(sq_added, i * 2 + s + 1)
                    copy_scaled(xf_hi[:, ds(i * 2 + s, 1), :].rearrange("p a t -> p (a t)"),
                                res[:, ds(i * 2 + s, 1), :].rearrange("p a t -> p (a t)"),
                                g2[:, ds(i * 2 + s, 1)]).then_inc(xf_hi_ready, 1)
                    nc.scalar.activation(tmp[:, s, :], res[:, ds(i * 2 + s, 1), :].rearrange("p a t -> p (a t)"),
                                         ACT.Square).then_inc(sq_ready, 1)
            def high_r(c, i, s):
                m = c * KT + i * 2 + s
                act.wait_ge(set_free[s], c * KT + i + JG // 2 + 2)
                nc.scalar.activation(tmp[:, s, :], tmp[:, s, :], ACT.Square).then_inc(r_ready, 1)
                act.wait_ge(r_ready, m + 1)
                copy(r_hi[:, ds(i * 2 + s, 1), :].rearrange("p a t -> p (a t)"), tmp[:, s, :]).then_inc(r_hi_ready, 1)

            def chunk(c, first, last):
                jh = c * KT + JG // 2
                if first:
                    split_hi(JG + 1, JG // 2, 1)
                    split_hi(JG + 2, JG // 2 + 1, 0)
                    high_r(c, 0, 0)
                    high_r(c, 0, 1)
                with act.Fori(int(first), KT // 2) as i:
                    for s in range(2):
                        split_hi(c * 2 * KT + i * 2 + JG + s + 1, jh + i + (s + 1) // 2, 1 - s)
                        high_r(c, i, s)
                with act.Fori(0, KT // 2 - last) as i:
                    for s in range(2):
                        split_hi(c * 2 * KT + i * 2 + JG + KT + s + 1, jh + i + (KT + s + 1) // 2, 1 - s)
                        if last:
                            act.wait_ge(y_sq_added, i * 2 + s + 1)
                            act.wait_ge(set_free[s], jh + i + KT // 2 + 2)
                            nc.scalar.activation(tmp[:, s, :], res[:, ds(i * 2 + s, 1), :].rearrange("p a t -> p (a t)"),
                                                 ACT.Square).then_inc(y_sq, 1)
                if last:
                    split_hi(JN - 1, JN // 2 - 1, 1)
                    for s in range(2):
                        act.wait_ge(y_sq_added, KT - 1 + s)
                        act.wait_ge(set_free[s], JN // 2 + 1)
                        nc.scalar.activation(tmp[:, s, :], res[:, KT - 2 + s, :], ACT.Square).then_inc(y_sq, 1)

            chunk(0, True, False)
            with act.Fori(1, NC - 1) as c:
                chunk(c, False, False)
            act.dma_start(gf_row[:, :], lnf_g.rearrange("(a n) -> a n", a=1).to_broadcast([P, D])).then_inc(gf_in, 16)
            chunk(NC - 1, False, True)

        @block.vector
        def _(dve):
            chain = Chain(dve, chain_v)
            tt, ts, cp = nc.vector.tensor_tensor, nc.vector.tensor_scalar, nc.vector.tensor_copy

            def split_lo(j, s):
                dve.wait_ge(w_hi_ready, j + 1)
                tt(w_lo[:, s], raw[:, s], w_hi[:, s].bitcast(F32), ALU.subtract).then_inc(w_split, 1)

            for t in range(NTOK):
                r = ROWS[t]
                dve.wait_ge(xg_done, t + 1)
                dve.wait_ge(rstd_spread, t + 1)
                x_ = xg[:, t % 2, :, 0:r]
                tt(x_, x_, ps[:, 6 + t % 2, 0:r].unsqueeze(1).to_broadcast([P, KT, r]), ALU.mult).then_inc(xn_ready, 1)
                dve.wait_ge(xhi_done, t + 1)
                tt(xn_lo[:, :, toks(t)], x_, xn_hi[:, :, toks(t)].bitcast(F32), ALU.subtract).then_inc(xn_done, 1)
                if t == NBLK - 4:
                    split_lo(0, 0)

            def bank_low(n):
                j, b = n // NT, n % NT
                cols = slice(b * TN, (b + 1) * TN)
                dve.wait_ge(bank_hi, n + 1)
                if j >= JB:
                    dve.sem_inc(bank_free, 1)
                    return
                par, g, pair = j // 3 % 2, j // 3, j % 3 - 1
                dec = slice(TN - NB, TN)
                for half in range(2):
                    rows = slice(half * HD, (half + 1) * HD)
                    if pair < 0:
                        last = tt(k_lo[par][rows, cols], ps[0:HD, b, 0:TN], k_hi[par][rows, cols].bitcast(F32), ALU.subtract)
                    else:
                        h = 2 * pair + half
                        last = tt(q_st[par][HD:P, h, cols], ps[rows, b, 0:TN], q_st[par][0:HD, h, cols].bitcast(F32), ALU.subtract)
                        if b == NT - 1:
                            last = cp(q_dec[:, :, g * HPG + h], ps[rows, b, dec])
                if pair < 0 and b == NT - 1:
                    cp(k_dec[:, g, :], ps[0:HD, b, dec])
                    last = cp(v_dec[:, g, :], ps[HD:P, b, dec])
                last.then_inc(bank_free, 1)

            def mask(u):
                slot, lo = u % 2, P if u % NBLK == 0 else 0
                dve.wait_ge(scores_ready, u + 1)
                if u >= 2:
                    dve.wait_ge(probs_turned, u - 1)
                if u % NBLK == 0:
                    dve.wait_ge(abias_ready, u // NBLK + 1)
                cp(prob[:, slot, :, 2 * P], nsink_g[:, :])
                for h in range(HPG):
                    c = (h % 2) * 2 * P
                    last = nc.vector.tensor_tensor_reduce(
                        out=prob[:, slot, h, lo:2 * P], in0=ps[:, 3 + 2 * slot + h // 2, c + lo:c + 2 * P],
                        in1=abias[:, h, lo:2 * P], scale=-SCALE, scalar=nsink_g[:, h:h + 1],
                        op0=ALU.add, op1=ALU.min, accum_out=nmax[:, slot, h:h + 1])
                last.then_inc(scores_masked, 1)

            def recip(u):
                dve.wait_ge(exp_done, u + 1)
                nc.vector.reciprocal(rden[:, u % 2, :], den[:, u % 2, :]).then_inc(rden_done, 1)

            def move_pt(u):
                dve.wait_ge(probs_turned, u + 1)
                if u >= 1:
                    dve.wait_ge(pv_done, u)
                if u % NBLK == 0:
                    dve.sem_inc(pt_v, 1)
                else:
                    cp(p_t[:, 0, :, :], ps[:, 3 + 2 * (u % 2), :].rearrange("p (h q) -> p h q", h=HPG)).then_inc(pt_v, 1)

            def move_v(g, n):
                dve.wait_ge(kv_turned, 3 * g + n + 1)
                if n == 1:
                    if g >= 1:
                        dve.wait_ge(tail_out, 64 * g)
                    cp(kv_tail[:, 0, :], ps[:, 7, 3 * P:4 * P]).then_inc(tail_ready, 1)
                for half in range(2):
                    last = cp(v_dup[g % 2][:, 4 * n:4 * n + 4, half * HD:(half + 1) * HD],
                              ps[:, 7, :].rearrange("p (t c) -> p t c", t=4)[:, :, HD:P])
                last.then_inc(v_moved, 1)

            split_lo(1, 1)
            dve.wait_ge(small_in, 48)
            ts(nsink[:, :], nsink[:, :], -1.0, None, ALU.mult).then_inc(nsink_ready, 1)
            for n in range(3 * NT):
                bank_low(n)
                if n in (2, 5):
                    split_lo(n // NT + 2, n // NT % 2)
            for u in range(NU):
                g, b = u // NBLK, u % NBLK
                n, j = (g + 1) * 3 * NT, (g + 1) * 3
                if b == 0:
                    mask(u)
                    recip(u)
                    bank_low(n)
                if b < NBLK - 1:
                    mask(u + 1)
                if b < 2:
                    move_v(g, b)
                if b == 2:
                    dve.wait_ge(kv_turned, 3 * g + 3)
                    cp(kv_tail[0:NB, 1, :], ps[0:NB, 7, 0:P]).then_inc(tail_ready, 1)
                move_pt(u)
                if b < NBLK - 1:
                    recip(u + 1)
                bank_low(n + b + 1)
                if b in (0, 2, 5):
                    w = j + {0: 1, 2: 2, 5: 3}[b]
                    split_lo(w, w % 2)

            split_lo(JB + 4, 0)
            dve.wait_ge(pv_done, NU)
            for col, row in ((slopes, slope_row), (nsink, nsink_row)):
                chain.link(tt(dself[:, :].rearrange("p (b h) -> p b h", b=NB), ident[:, :].rearrange("p (b h) -> p b h", b=NB),
                              col[:, :].unsqueeze(1).to_broadcast([P, NB, H]), ALU.mult))
                chain.link(nc.vector.reduce_sum(row[:, :], dself[:, :], axis=mybir.AxisListType.X))
            dve.wait_ge(dbias_ready, 1)
            ts(dbias[:, :], dbias[:, :], slope_row[:, 0:1], None, ALU.mult)
            cp(dprob[:, W + 1:W + 2], nsink_row[:, :])
            tt(prod_t[:, :, :].rearrange("p b (g h) -> p b g h", g=NG), q_dec[:, :, :].rearrange("p b (g h) -> p b g h", g=NG),
               k_dec[:, :, :].rearrange("p g b -> p b g").unsqueeze(3).to_broadcast([HD, NB, NG, HPG]),
               ALU.mult).then_inc(dprod_ready, 1)
            split_lo(JB + 5, 1)
            dve.wait_ge(dst_done, NB)
            cp(st_sb[:, :], ps[:, 5, 0:P]).then_inc(dst_moved, 1)
            split_lo(JB + 6, 0)
            dve.wait_ge(ds_ready, 1)
            nc.vector.tensor_tensor_reduce(out=dprob[:, 0:W + 1], in0=ps[:, 4, 0:W + 1], in1=dbias[:, :],
                                           scale=-SCALE, scalar=nsink_row[:, 0:1], op0=ALU.add, op1=ALU.min,
                                           accum_out=dstat[:, 0:1]).then_inc(dmasked, 1)
            dve.wait_ge(dexp, 1)
            chain.link(nc.vector.reciprocal(dstat[:, 2:3], dstat[:, 1:2]))
            chain.link(ts(dprob[:, 0:W + 1], dprob[:, 0:W + 1], dstat[:, 2:3], None, ALU.mult))
            ts(dself[:, :], ident[:, :], dprob[:, W:W + 1], None, ALU.mult).then_inc(dprobs, 1)
            split_lo(JB + 7, 1)
            dve.wait_ge(dp_turned, 1)
            cp(dp_t[:, :, :].rearrange("p b h -> p (b h)"), ps[:, 3, 0:P]).then_inc(dp_moved, 1)
            dve.wait_ge(dpv_done, 1)
            vb = v_dec[:, :, :].rearrange("p g b -> p b g").unsqueeze(3).to_broadcast([HD, NB, NG, HPG])
            chain.link(tt(d_o[:, :, :].rearrange("p b (g h) -> p b g h", g=NG),
                          ps[0:HD, 7, 0:P].rearrange("p (b g h) -> p b g h", b=NB, g=NG), vb, ALU.mult))
            flat = d_o[:, :, :].rearrange("p b h -> p (b h)")
            chain.link(tt(flat, ps[0:HD, 6, 0:P], flat, ALU.add))
            for par in range(2):
                last = cp(b_all[par * HD:(par + 1) * HD, :, SEQ:T], d_o[:, :, :].rearrange("p b (t r) -> p r t b", r=2)[:, par])
            last.then_inc(db_ready, 1)
            split_lo(JW, 0)
            for k in range(KT):
                dve.wait_ge(b_hi_ready, k + 1)
                tt(b_lo[:, k, :], b_all[:, k, :], b_hi[:, k, :].bitcast(F32), ALU.subtract).then_inc(b_split, 1)

            dve.wait_ge(gate_free, (JW - JB - 3) * NT)
            with dve.Fori(0, KT // 2) as i:
                chain.enter(i, 4)
                for s in range(2):
                    j = i * 2 + JW + s
                    split_lo(j + 1, 1 - s)
                    hn = h_f[:, ds(i * 2 + s, 1), :].rearrange("p a t -> p (a t)")
                    dve.wait_ge(set_free[s], i + JW // 2 + 1)
                    chain.link(ts(tmp[:, s, :], hn, 1.0, None, ALU.add))
                    chain.link(nc.vector.reciprocal(tmp[:, s, :], tmp[:, s, :]))
                    dve.wait_ge(job_done, j + 2)
                    tt(by3(hn), by3(tmp[:, s, :]), pset(s), ALU.mult).then_inc(set_free[s], 1)
            chain.leave(KT // 2)

            def variances(bank):
                ts(var[:, 0:NBLK], ps[:, bank, 0:NBLK], 1.0 / D, EPS, ALU.mult, ALU.add)
                return ts(var[0:NB, NBLK:], ps[0:NB, bank, NBLK:NTOK], 1.0 / D, EPS, ALU.mult, ALU.add)

            dve.wait_ge(set_free[1], JC // 2 + 1)
            with dve.Fori(0, KT // 2) as i:
                for s in range(2):
                    split_lo(i * 2 + JC + s + 1, 1 - s)
                    dve.wait_ge(set_free[s], i + JC // 2 + 2)
                    dve.wait_ge(v_sq_added, i * 2 + s + 1)
                    v_ = mix[:, ds(i * 2 + s, 1), :].rearrange("p a t -> p (a t)")
                    tt(tmp[:, s, :], v_, v_, ALU.mult).then_inc(v_sq, 1)
            dve.wait_ge(sgu_in, 64)
            tt(wt_dec[:, :, :], ident[0:NB, 0:NB].unsqueeze(1).to_broadcast([NB, GS, NB]),
               wt00[:, :].unsqueeze(2).to_broadcast([NB, GS, NB]), ALU.mult)
            dve.wait_ge(wt_turned, 1)
            cp(wt[:, :, :], ps[:, 6:8, :].rearrange("p a (g q) -> p (a g) q", q=P)).then_inc(wt_ready, 1)

            def scale_mix(t):
                r, bank = ROWS[t], 4 + 2 * (t % 2)
                dve.wait_ge(mixed, t + 1)
                tt(mix[:, :, toks(t)], ps[:, bank:bank + 2, :].rearrange("p a (k q) -> p (a k) q", q=P)[:, :, 0:r],
                   gv[:, :].unsqueeze(2).to_broadcast([P, KT, r]), ALU.mult).then_inc(scaled, 1)

            dve.wait_ge(v_ss, 1)
            variances(6).then_inc(v_var, 1)
            for t in range(NTOK):
                scale_mix(t)
            dve.wait_ge(vn_ready, NTOK)
            tt(vs_out[:, :], vn[0:NB, NBLK % 2, :], gv_row[:, :], ALU.mult).then_inc(vs_ready, 1)

            dve.wait_ge(mix_ready, NTOK)
            dve.wait_ge(vs_stored, 16)
            with dve.Fori(0, KT // 2) as i:
                for s in range(2):
                    n = i * 2 + s
                    split_lo(i * 2 + JD + s + 1, 1 - s)
                    dve.wait_ge(set_free[s], i + JD // 2 + 2)
                    tt(tmp[:, s, :], tmp[:, s, :], mix[:, ds(n, 1), :].rearrange("p a t -> p (a t)"), ALU.mult).then_inc(a_ready, 1)
                    dve.wait_ge(a_hi_ready, n + 1)
                    tt(a_lo[:, ds(n, 1), :].rearrange("p a t -> p (a t)"), tmp[:, s, :],
                       a_hi[:, ds(n, 1), :].rearrange("p a t -> p (a t)").bitcast(F32), ALU.subtract).then_inc(a_lo_ready, 1)

            def gated(n):
                dve.wait_ge(set_free[0], n + JE // 2 + 2)
                dve.wait_ge(h_ready, n + 1)
                dve.wait_ge(job_done, n * 2 + JE + 3)
                tt(by3(tmp[:, 1, :]), by3(tmp[:, 0, :]), pset(1), ALU.mult).then_inc(set_free[1], 1)

            def low_h(n):
                dve.wait_ge(h_hi_ready, n + 1)
                tt(h_lo[:, n, :], h_f[:, n, :], h_hi[:, n, :].bitcast(F32), ALU.subtract).then_inc(h_split, 1)

            with dve.Fori(0, KT - 1) as n:
                j = n * 2 + JE
                split_lo(j + 1, 1)
                split_lo(j + 2, 0)
                gated(n)
            split_lo(JF - 1, 1)
            split_lo(JF, 0)
            for n in range(KT - 1):
                low_h(n)
            gated(KT - 1)

            low_h(KT - 1)

            def add_res(n, s):
                r_ = by3(res[:, ds(n, 1), :].rearrange("p a t -> p (a t)"))
                tt(r_, pset(s), r_, ALU.add).then_inc(set_free[s], 1)

            with dve.Fori(0, KT // 2) as i:
                for s in range(2):
                    j = i * 2 + JF + s
                    split_lo(j + 1, 1 - s)
                    dve.wait_ge(res_in[0], 16)
                    dve.wait_ge(res_in[1], 16)
                    dve.wait_ge(job_done, j + 2)
                    add_res(i * 2 + s, s)
                    dve.wait_ge(xf_hi_ready, i * 2 + s + 1)
                    nc.vector.scalar_tensor_tensor(
                        out=xf_lo[:, ds(i * 2 + s, 1), :].rearrange("p a t -> p (a t)"),
                        in0=res[:, ds(i * 2 + s, 1), :].rearrange("p a t -> p (a t)"), scalar=g2[:, ds(i * 2 + s, 1)],
                        in1=xf_hi[:, ds(i * 2 + s, 1), :].rearrange("p a t -> p (a t)").bitcast(F32),
                        op0=ALU.mult, op1=ALU.subtract).then_inc(xf_split, 1)
            split_lo(JG + 1, 1)
            dve.wait_ge(ss_ready, 1)
            variances(6).then_inc(var_ready, 1)
            split_lo(JG + 2, 0)
            for n, (bank, t0, t1) in enumerate(RB):
                dve.wait_ge(rb_ready, n + 1)
                w_ = min(t1 * P, T) - t0 * P
                cp(rstd_b[:, t0 * P:t0 * P + w_], ps[:, bank, 0:w_]).then_inc(rb_moved, 1)
            dve.wait_ge(rb_moved, len(RB))

            def low_r(c, i, s):
                j, m = c * 2 * KT + i * 2 + JG + s, c * KT + i * 2 + s
                dve.wait_ge(job_done, j + 2)
                dve.wait_ge(r_split, m + 1)
                nc.vector.scalar_tensor_tensor(
                    out=by3(tmp[:, s, :]), in0=pset(s), scalar=0.0, in1=by3(rstd_b[:, :]),
                    op0=ALU.max, op1=ALU.mult).then_inc(set_free[s], 1)
                dve.wait_ge(r_hi_ready, m + 1)
                tt(r_lo[:, ds(i * 2 + s, 1), :].rearrange("p a t -> p (a t)"), tmp[:, s, :],
                   r_hi[:, ds(i * 2 + s, 1), :].rearrange("p a t -> p (a t)").bitcast(F32),
                   ALU.subtract).then_inc(r_split, 1)

            def chunk(c, first, last):
                if first:
                    low_r(c, 0, 0)
                    low_r(c, 0, 1)
                with dve.Fori(int(first), KT // 2) as i:
                    for s in range(2):
                        split_lo(c * 2 * KT + i * 2 + JG + s + 1, 1 - s)
                        low_r(c, i, s)
                with dve.Fori(0, KT // 2 - last) as i:
                    for s in range(2):
                        j = c * 2 * KT + i * 2 + JG + KT + s
                        split_lo(j + 1, 1 - s)
                        dve.wait_ge(job_done, j + 2)
                        add_res(i * 2 + s, s)
                if last:
                    split_lo(JN - 1, 1)
                    for s in range(2):
                        dve.wait_ge(job_done, JN + s)
                        add_res(KT - 2 + s, s)

            chunk(0, True, False)
            with dve.Fori(1, NC - 1) as c:
                chunk(c, False, False)
            chunk(NC - 1, False, True)
            dve.wait_ge(y_ss, 1)
            variances(6).then_inc(y_var, 1)
            dve.wait_ge(gf_in, 16)
            dve.wait_ge(y_rstd, 1)
            for t in range(NTOK):
                r, bank = ROWS[t], 2 * (t % 3)
                dve.wait_ge(y_turned, t + 1)
                if t >= YS:
                    dve.wait_ge(y_stored[t % YS], 16 * (t // YS))
                nc.vector.scalar_tensor_tensor(
                    out=y_t[0:r, t % YS, :].rearrange("p (a b) -> p a b", a=2), in0=ps[0:r, bank:bank + 2, :],
                    scalar=rstd[0:r, t:t + 1], in1=gf_row[0:r, :].rearrange("p (a b) -> p a b", a=2),
                    op0=ALU.mult, op1=ALU.mult).then_inc(y_ready, 1)

        @block.tensor
        def _(pe):
            mm = nc.tensor.matmul

            def turn(out, in_, r=P):
                return nc.tensor.transpose(out, in_, ident[0:r, 0:r])

            def job(j, h, s, hi, lo, ready=None, banks_first=False):
                pe.wait_ge(w_split, j + 3)
                pe.wait_ge(set_free[s], h + 1)
                passes = ((w_hi, hi), (w_hi, lo), (w_lo, hi))
                order = [(k, n, b) for k in range(KT) for n in range(3) for b in range(NT)]
                if banks_first:
                    order = [(k, n, b) for b in range(NT) for k in range(KT) for n in range(3)]
                seen = None
                for k, n, b in order:
                    at_ = b if banks_first else k
                    if ready and at_ != seen:
                        ready(at_)
                        seen = at_
                    w, x = passes[n]
                    last = mm(ps[:, 3 * s + b, 0:TN], w[:, s, k, :], x[:, k, b * TN:(b + 1) * TN],
                              start=(k == 0 and n == 0), stop=(k == KT - 1 and n == 2))
                last.then_inc(job_done, 1)

            def bank(j, n, s, b, ready=None):
                if b == 0:
                    pe.wait_ge(w_split, j + 3)
                if ready is not None:
                    pe.wait_ge(xn_done, ready)
                if n is not None:
                    pe.wait_ge(bank_free, n + 1)
                for k in range(KT):
                    for p, (w, x) in enumerate(((w_hi, xn_hi), (w_hi, xn_lo), (w_lo, xn_hi))):
                        last = mm(ps[:, b, 0:TN], w[:, s, k, :], x[:, k, b * TN:(b + 1) * TN],
                                  start=(k == 0 and p == 0), stop=(k == KT - 1 and p == 2))
                last.then_inc(bank_done if b < NT - 1 else job_done, 1)

            def spread_rstd(place_, t):
                r = ROWS[t]
                return mm(place_, rstd[0:r, t:t + 1].to_broadcast([r, P]), ident[0:r, 0:r], start=True, stop=True)

            pe.wait_ge(const_ready, 1)

            def spread(t):
                pe.wait_ge(rstd_done, t + 1)
                if t >= 2:
                    pe.wait_ge(xn_ready, t - 1)
                spread_rstd(ps[:, 6 + t % 2, 0:ROWS[t]], t).then_inc(rstd_spread, 1)

            for t in range(NTOK):
                r, first = ROWS[t], 2 * (t % 3)
                pe.wait_ge(x_in[t], 16)
                if t >= 3:
                    spread(t - 3)
                    pe.wait_ge(xt_moved, t - 2)
                for k in range(KT):
                    last = turn(ps[:, first + k // 4, (k % 4) * P:(k % 4) * P + r], x_stage[0:r, t, k * P:(k + 1) * P], r)
                last.then_inc(xt_done, 1)
            spread(NTOK - 3)
            pe.wait_ge(xt_moved, NTOK - 2)
            bank(0, 0, 0, 0, ready=3)
            spread(NTOK - 2)
            spread(NTOK - 1)
            pe.wait_ge(xt_moved, NTOK)

            def scores(u, n0, par, b):
                lo, slot = P if b == 0 else 0, b % 2
                if b in (0, 2, 5):
                    pe.wait_ge(bank_free, n0 + NT + 6 + ((b + 1) * P - 1) // TN + 1)
                pe.wait_ge(pt_a, u + 1)
                pe.wait_ge(pt_v, u + 1)
                keys = slice((b - 1) * P + lo, (b + 1) * P)
                for h in range(HPG):
                    c = (h % 2) * 2 * P
                    for n, k_ in enumerate((k_hi[par], k_lo[par])):
                        last = mm(ps[:, 3 + 2 * slot + h // 2, c + lo:c + 2 * P], q_st[par][:, h, b * P:(b + 1) * P],
                                  k_[:, keys], start=(n == 0), stop=(n == 1))
                last.then_inc(scores_ready, 1)

            def turn_probs(u, b):
                pe.wait_ge(probs_ready, u + 1)
                for kb in range(1 if b == 0 else 0, 2):
                    for h in range(HPG):
                        last = turn(ps[:, 3 + 2 * (b % 2) + kb, h * P:(h + 1) * P], prob[:, b % 2, h, kb * P:(kb + 1) * P])
                last.then_inc(probs_turned, 1)

            def values(u, par, b):
                pe.wait_ge(pt_a, u + 3)
                pe.wait_ge(pt_v, u + 3)
                pe.wait_ge(o_moved, u + 1)
                first = 1 if b == 0 else 0
                for kb in range(first, 2):
                    last = mm(ps[:, 7, :], v_dup[par][:, b - 1 + kb, :], p_t[:, kb, :, :].rearrange("p h q -> p (h q)"),
                              start=(kb == first), stop=(kb == 1))
                last.then_inc(pv_done, 1)

            for n in range(1, 3 * NT):
                b = n % NT
                bank(n // NT, n, n // NT % 2, b, ready=min(NTOK, -(-(b + 1) * TN // P)))
            with pe.Fori(0, NG // 2) as gp:
                for par in range(2):
                    g, u0 = gp * 2 + par, gp * 2 * NBLK + par * NBLK
                    n0 = gp * 6 * NT + par * 3 * NT

                    def next_bank(m):
                        bank(gp * 6 + 3 * par + 3 + m // NT, n0 + 3 * NT + m, (par + 1 + m // NT) % 2, m % NT)

                    scores(u0, n0, par, 0)
                    next_bank(0)
                    for b in range(NBLK):
                        if b + 1 < NBLK:
                            scores(u0 + b + 1, n0, par, b + 1)
                        if b < 2:
                            pe.wait_ge(o_moved, u0 + b + 1)
                            for t in range(4):
                                last = turn(ps[:, 7, t * P:(t + 1) * P], kv_t[par][:, (4 * b + t) * P:(4 * b + t + 1) * P])
                            last.then_inc(kv_turned, 1)
                        if b == 2:
                            pe.wait_ge(o_moved, u0 + b + 1)
                            turn(ps[0:NB, 7, 0:P], kv_t[par][:, SEQ:T]).then_inc(kv_turned, 1)
                        turn_probs(u0 + b, b)
                        next_bank(b + 1)
                        if b < 2:
                            pe.wait_ge(v_moved, g * 2 + b + 1)
                        if b == 2:
                            pe.wait_ge(tail_ready, g * 2 + 2)
                        values(u0 + b, par, b)

            def gate_bank(m):
                if m < NT:
                    pe.wait_ge(bank_free, NS + m + 1)
                else:
                    pe.wait_ge(gate_free, m - NT + 1)
                n = NS + m
                bank(n // NT, None, n // NT % 2, n % NT)

            gate_bank(0)
            gate_bank(1)
            pe.wait_ge(cache_in, 32)
            pe.wait_ge(o_moved, NU + 1)
            for b in range(NB + 1):
                if b < NB:
                    if b >= 2:
                        pe.wait_ge(dk_moved, b - 1)
                    for g in range(NG):
                        last = turn(ps[0:HD, 6 + b % 2, g * P:(g + 1) * P], ck[:, b, g * HD:(g + 1) * HD])
                    last.then_inc(dk_turned, 1)
                if b >= 1:
                    pe.wait_ge(dk_moved, b)
                    for g in range(NG):
                        c = (b - 1) * H + g * HPG
                        last = mm(ps[:, 5, c:c + HPG], ck_t[:, (b - 1) % 2, g, :], q_dec[:, b - 1, g * HPG:(g + 1) * HPG],
                                  start=True, stop=True)
                    last.then_inc(dst_done, 1)
                if b % 2 == 1:
                    gate_bank(2 + b // 2)
            gate_bank(6)
            pe.wait_ge(dst_moved, 1)
            pe.wait_ge(dprod_ready, 1)
            turn(ps[:, 4, 0:P], st_sb[:, :])
            mm(ps[:, 4, P:P + 1], prod_t[:, :, :].rearrange("p b h -> p (b h)"), ones[0:HD, 0:1],
               start=True, stop=True).then_inc(ds_ready, 1)
            gate_bank(7)
            gate_bank(8)
            pe.wait_ge(dprobs, 1)
            turn(ps[:, 3, 0:P], dprob[:, 0:W])
            mm(ps[0:HD, 7, 0:P], ones[:, 0:HD], dself[:, :], start=True, stop=True).then_inc(dp_turned, 1)
            gate_bank(9)
            pe.wait_ge(dp_moved, 1)
            for b in range(NB):
                for g in range(NG):
                    c = b * H + g * HPG
                    last = mm(ps[0:HD, 6, c:c + HPG], cv[:, b, g * HD:(g + 1) * HD], dp_t[:, b, g * HPG:(g + 1) * HPG],
                              start=True, stop=True)
            last.then_inc(dpv_done, 1)
            for m in range(10, 15):
                gate_bank(m)
            pe.wait_ge(gate_free, 15)
            with pe.Fori(0, KT // 2) as i:
                for s in range(2):
                    job(i * 2 + JW + s, i + JW // 2, s, b_hi, b_lo, lambda k: pe.wait_ge(b_split, k + 1))
            with pe.Fori(0, KT // 2 - 1) as i:
                for s in range(2):
                    job(i * 2 + JC + s, i + JC // 2, s, xn_hi, xn_lo)
            pe.wait_ge(sgu_masked, 1)
            for g in range(GS):
                last = turn(ps[:, 6 + g // 4, (g % 4) * P:(g % 4 + 1) * P], sgu_raw[:, g, :])
            last.then_inc(wt_turned, 1)
            for s in range(2):
                job(JD - 2 + s, JD // 2 - 1, s, xn_hi, xn_lo)
            for s in range(2):
                pe.wait_ge(set_free[s], JD // 2 + 1)

            def sums(bank, added, squared):
                pe.wait_ge(added, KT + 1)
                pe.wait_ge(squared, KT)
                for t in range(NTOK):
                    mm(ps[0:ROWS[t], bank, t:t + 1], sq_sum[:, toks(t)], ones[:, 0:1], start=True, stop=False)
                    last = mm(ps[0:ROWS[t], bank, t:t + 1], tmp[:, 1, toks(t)], ones[:, 0:1], start=False, stop=True)
                return last

            def turn_v(t):
                r, bank = ROWS[t], 2 * (t % 2)
                if t >= 2:
                    pe.wait_ge(vn_ready, t - 1)
                for k in range(KT):
                    last = turn(ps[0:r, bank + k // 4, (k % 4) * P:(k % 4 + 1) * P], mix[:, k, toks(t)])
                last.then_inc(vt_turned, 1)

            turn_v(0)
            pe.wait_ge(wt_ready, 1)
            sums(6, v_sq_added, v_sq).then_inc(v_ss, 1)
            turn_v(1)
            pe.wait_ge(v_var, 1)
            for t in range(NTOK):
                r, bank = ROWS[t], 4 + 2 * (t % 2)
                pe.wait_ge(vn_ready, t + 1)
                if t >= 2:
                    pe.wait_ge(scaled, t - 1)
                for g in range(GS):
                    w_ = wt[:, g, :] if t < NBLK else wt_dec[:, g, :]
                    last = mm(ps[:, bank + g // 4, (g % 4) * P:(g % 4) * P + r], vn[0:r, t % 2, g * P:(g + 1) * P], w_,
                              start=True, stop=True)
                last.then_inc(mixed, 1)
                if t + 2 < NTOK:
                    turn_v(t + 2)
            pe.wait_ge(scaled, NTOK)
            with pe.Fori(0, KT // 2) as i:
                for s in range(2):
                    job(i * 2 + JD + s, i + JD // 2, s, xn_hi, xn_lo)
            with pe.Fori(0, KT) as n:
                job(n * 2 + JE, n + JE // 2, 0, xn_hi, xn_lo)
                pe.wait_ge(a_lo_ready, KT + 2)
                job(n * 2 + JE + 1, n + JE // 2, 1, a_hi, a_lo)
            with pe.Fori(0, KT // 2) as i:
                for s in range(2):
                    job(i * 2 + JF + s, i + JF // 2, s, h_hi, h_lo, lambda k: pe.wait_ge(h_split, k + 1))
            def up(c, i, s, wait=True):
                job(c * 2 * KT + i * 2 + JG + s, c * KT + i + JG // 2, s, xf_hi, xf_lo,
                    (lambda k: pe.wait_ge(xf_split, k + 1)) if wait else None)

            def down(c):
                with pe.Fori(0, KT // 2) as i:
                    for s in range(2):
                        job(c * 2 * KT + i * 2 + JG + KT + s, c * KT + i + (JG + KT) // 2, s, r_hi, r_lo,
                            lambda k: pe.wait_ge(r_split, c * KT + k + 3))

            up(0, 0, 0)
            sums(6, sq_added, sq_ready).then_inc(ss_ready, 1)
            up(0, 0, 1, False)
            pe.wait_ge(rs_ready, 1)
            for n, (bank, t0, t1) in enumerate(RB):
                if n >= 2:
                    pe.wait_ge(rb_moved, n - 1)
                for t in range(t0, t1):
                    last = spread_rstd(ps[:, bank, (t - t0) * P:(t - t0) * P + ROWS[t]], t)
                last.then_inc(rb_ready, 1)
            with pe.Fori(1, KT // 2) as i:
                for s in range(2):
                    up(0, i, s, False)
            down(0)
            with pe.Fori(1, NC) as c:
                with pe.Fori(0, KT // 2) as i:
                    for s in range(2):
                        up(c, i, s, False)
                down(c)
            for s in range(2):
                pe.wait_ge(set_free[s], JN // 2 + 1)
            for t in range(NTOK):
                r, bank = ROWS[t], 2 * (t % 3)
                if t >= 3:
                    pe.wait_ge(y_ready, t - 2)
                for k in range(KT):
                    last = turn(ps[0:r, bank + k // 4, (k % 4) * P:(k % 4 + 1) * P], res[:, k, toks(t)])
                last.then_inc(y_turned, 1)
                if t == 2:
                    sums(6, y_sq_added, y_sq).then_inc(y_ss, 1)


_INS = ["x_prompt", "x_sample", "cache_k_win", "cache_v_win", "ln1_g", "w_in", "sgu_norm_g", "sgu_w", "sgu_b",
        "attn_sinks", "w_oa", "w_ob", "w_out", "ln2_g", "w_up", "w_down", "lnf_g"]


def kernel(**inputs):
    import numpy as np
    import concourse.bacc as bacc
    from concourse.bass_utils import run_bass_kernel_spmd

    nc = bacc.Bacc("TRN2", target_bir_lowering=False, num_devices=1)
    arrays, ins = {}, []
    for name in _INS:
        a = np.ascontiguousarray(inputs[name])
        arrays["in_" + name] = a
        ins.append(nc.dram_tensor("in_" + name, a.shape, mybir.dt.from_np(a.dtype), kind="ExternalInput").ap())
    xp, xs, ck = (arrays["in_" + n].shape for n in ("x_prompt", "x_sample", "cache_k_win"))
    window = min(ck[2], xp[1])
    shapes = [("y_prompt", xp), ("y_sample", xs),
              ("k_win_p", (ck[0], xp[0], window) + ck[3:]), ("v_win_p", (ck[0], xp[0], window) + ck[3:]),
              ("k_win_s", ck), ("v_win_s", ck), ("sgu_v_s", (ck[0],) + xs)]
    outs = [nc.dram_tensor("out_" + name, shape, F32, kind="ExternalOutput").ap() for name, shape in shapes]
    x_keep = nc.dram_tensor("x_keep", (xp[2], xp[1] + xs[0]), F32, kind="Internal").ap()
    build_trunk(nc, *ins, *outs, x_keep)
    r = run_bass_kernel_spmd(nc, [arrays], core_ids=[0])
    return tuple(r.results[0]["out_" + name] for name, _ in shapes)
```
